# Optimizing a Trainium2 kernel written in Bass

```python
import math
import jax, jax.numpy as jnp
from jax import lax
import numpy as np

D_MODEL = 1024
BATCH = 1
SEQ = 512
DEPTH = 2

CHUNK = 64
HEAD_DIM = 64
ROPE_THETA = 10000.0
EPS = 1e-6
NEG = -1e30

SWA_WINDOW = 128
SWA_CHUNKS = SWA_WINDOW // CHUNK
SWA_Q_HEADS = 8
SWA_KV_HEADS = 2
SWA_GROUP = SWA_Q_HEADS // SWA_KV_HEADS
SWA_WIDTH = SWA_Q_HEADS * HEAD_DIM
SWA_KV_WIDTH = SWA_KV_HEADS * HEAD_DIM

SSM_WIDTH = 256
SSM_GROUP_CH = 16
SSM_GROUPS = SSM_WIDTH // SSM_GROUP_CH
SSM_STATE = 64
SSM_DT_MIN = 1e-3
SSM_DT_MAX = 1e-1

FOX_HEADS = 4
FOX_WIDTH = FOX_HEADS * HEAD_DIM
FOX_BLOCK = 128

MIX_WIDTH = SWA_WIDTH + SSM_WIDTH + FOX_WIDTH
D_FF = 2816

IN_SIZES = (SWA_WIDTH, SWA_KV_WIDTH, SWA_KV_WIDTH, SSM_WIDTH, FOX_WIDTH, FOX_WIDTH, FOX_WIDTH, FOX_HEADS)
IN_WIDTH = sum(IN_SIZES)
IN_SPLITS = tuple(int(s) for s in np.cumsum(IN_SIZES)[:-1])
MIX_SPLITS = (SWA_WIDTH, SWA_WIDTH + SSM_WIDTH)

kernel_name = "hymba_swa_s5_fox_macaron_trunk"

def rms_norm(x, g):
    xf = x.astype(jnp.float32)
    y = xf * lax.rsqrt(jnp.mean(xf * xf, axis=-1, keepdims=True) + EPS)
    return (y * g.astype(jnp.float32)).astype(x.dtype)

def swiglu(x, w_gate, w_up, w_down):
    return (jax.nn.silu(x @ w_gate) * (x @ w_up)) @ w_down

def rope_tables(seq):
    pos = jnp.arange(seq, dtype=jnp.float32)
    inv = ROPE_THETA ** (-jnp.arange(0, HEAD_DIM, 2, dtype=jnp.float32) / HEAD_DIM)
    ang = pos[:, None] * inv[None, :]
    return jnp.cos(ang), jnp.sin(ang)

def apply_rope(x, cos, sin):
    xf = x.astype(jnp.float32)
    x1, x2 = jnp.split(xf, 2, axis=-1)
    c = cos[None, :, None, :]
    s = sin[None, :, None, :]
    return jnp.concatenate([x1 * c - x2 * s, x2 * c + x1 * s], axis=-1).astype(x.dtype)

def shift_chunks(t, o):
    if o == 0:
        return t
    return jnp.concatenate([jnp.zeros_like(t[:, :o]), t[:, :-o]], axis=1)

def swa_sink_attention(q, k, v, sinks, cos, sin):
    bsz, seq = q.shape[0], q.shape[1]
    nc = seq // CHUNK
    q = apply_rope(q.reshape(bsz, seq, SWA_Q_HEADS, HEAD_DIM), cos, sin)
    k = apply_rope(k.reshape(bsz, seq, SWA_KV_HEADS, HEAD_DIM), cos, sin)
    q = q.reshape(bsz, nc, CHUNK, SWA_KV_HEADS, SWA_GROUP, HEAD_DIM)
    kc = k.reshape(bsz, nc, CHUNK, SWA_KV_HEADS, HEAD_DIM)
    vc = v.reshape(bsz, nc, CHUNK, SWA_KV_HEADS, HEAD_DIM)
    offsets = range(SWA_CHUNKS - 1, -1, -1)
    kb = jnp.concatenate([shift_chunks(kc, o) for o in offsets], axis=2)
    vb = jnp.concatenate([shift_chunks(vc, o) for o in offsets], axis=2)
    key_off = jnp.repeat(jnp.arange(SWA_CHUNKS - 1, -1, -1), CHUNK)
    valid = (jnp.arange(nc)[:, None] - key_off[None, :]) >= 0
    s = jnp.einsum('bnqhgd,bnkhd->bnhgqk', q, kb).astype(jnp.float32) * (HEAD_DIM ** -0.5)
    s = jnp.where(valid[None, :, None, None, None, :], s, NEG)
    sink = jnp.broadcast_to(
        sinks.astype(jnp.float32).reshape(1, 1, SWA_KV_HEADS, SWA_GROUP, 1, 1), s.shape[:-1] + (1,))
    p = jax.nn.softmax(jnp.concatenate([s, sink], axis=-1), axis=-1)[..., :-1]
    o = jnp.einsum('bnhgqk,bnkhd->bnqhgd', p.astype(vb.dtype), vb)
    return o.reshape(bsz, seq, SWA_WIDTH)

def _complex_affine_combine(e1, e2):
    a1r, a1i, b1r, b1i = e1
    a2r, a2i, b2r, b2i = e2
    ar = a2r * a1r - a2i * a1i
    ai = a2r * a1i + a2i * a1r
    br = a2r * b1r - a2i * b1i + b2r
    bi = a2r * b1i + a2i * b1r + b2i
    return (ar, ai, br, bi)

def s5_mixer(u, lam_re, lam_im, log_dt, b_re, b_im, c_re, c_im, d_skip, glu_w, glu_b):
    bsz, seq = u.shape[0], u.shape[1]
    f32 = jnp.float32
    uf = u.astype(f32).reshape(bsz, seq, SSM_GROUPS, SSM_GROUP_CH)
    lr = jnp.minimum(lam_re.astype(f32), -1e-4)
    li = lam_im.astype(f32)
    dt = jnp.exp(log_dt.astype(f32))[:, None]
    mag = jnp.exp(lr * dt)
    ab_re = mag * jnp.cos(li * dt)
    ab_im = mag * jnp.sin(li * dt)
    den = lr * lr + li * li
    nr = ab_re - 1.0
    ni = ab_im
    z_re = (nr * lr + ni * li) / den
    z_im = (ni * lr - nr * li) / den
    br, bi = b_re.astype(f32), b_im.astype(f32)
    bb_re = z_re[..., None] * br - z_im[..., None] * bi
    bb_im = z_re[..., None] * bi + z_im[..., None] * br
    bu_re = jnp.einsum('gpc,bsgc->bsgp', bb_re, uf)
    bu_im = jnp.einsum('gpc,bsgc->bsgp', bb_im, uf)
    a_re = jnp.broadcast_to(ab_re, bu_re.shape)
    a_im = jnp.broadcast_to(ab_im, bu_im.shape)
    _, _, h_re, h_im = lax.associative_scan(_complex_affine_combine, (a_re, a_im, bu_re, bu_im), axis=1)
    y = (jnp.einsum('gcp,bsgp->bsgc', c_re.astype(f32), h_re)
         - jnp.einsum('gcp,bsgp->bsgc', c_im.astype(f32), h_im))
    y = y.reshape(bsz, seq, SSM_WIDTH) + d_skip.astype(f32) * uf.reshape(bsz, seq, SSM_WIDTH)
    y = jax.nn.gelu(y)
    y = y * jax.nn.sigmoid(y @ glu_w.astype(f32) + glu_b.astype(f32))
    return y.astype(u.dtype)

def fox_attention(q, k, v, f_logit, f_bias):
    bsz, seq = q.shape[0], q.shape[1]
    nb = seq // FOX_BLOCK
    q = q.reshape(bsz, seq, FOX_HEADS, HEAD_DIM)
    k = k.reshape(bsz, seq, FOX_HEADS, HEAD_DIM)
    v = v.reshape(bsz, seq, FOX_HEADS, HEAD_DIM)
    logf = jax.nn.log_sigmoid(f_logit.astype(jnp.float32) + f_bias.astype(jnp.float32))
    cum = jnp.cumsum(logf, axis=1)
    cum_k = cum.transpose(0, 2, 1)
    qb = q.reshape(bsz, nb, FOX_BLOCK, FOX_HEADS, HEAD_DIM).transpose(1, 0, 2, 3, 4)
    cb = cum.reshape(bsz, nb, FOX_BLOCK, FOX_HEADS).transpose(1, 0, 3, 2)
    key_pos = jnp.arange(seq)
    scale = HEAD_DIM ** -0.5

    def block(args):
        q_blk, c_blk, i = args
        s = jnp.einsum('bqhd,bkhd->bhqk', q_blk, k).astype(jnp.float32) * scale
        s = s + c_blk[..., None] - cum_k[:, :, None, :]
        q_pos = i * FOX_BLOCK + jnp.arange(FOX_BLOCK)
        s = jnp.where(key_pos[None, :] <= q_pos[:, None], s, NEG)
        p = jax.nn.softmax(s, axis=-1).astype(v.dtype)
        return jnp.einsum('bhqk,bkhd->bqhd', p, v)

    out = lax.map(block, (qb, cb, jnp.arange(nb)))
    return out.transpose(1, 0, 2, 3, 4).reshape(bsz, seq, FOX_WIDTH)

def hybrid_mixer(u, w_in, swa_sinks, lam_re, lam_im, log_dt, b_re, b_im, c_re, c_im,
                 d_skip, glu_w, glu_b, fox_f_bias, mix_gain, w_out, cos, sin):
    proj = u @ w_in
    qa, ka, va, us, qc, kc, vc, fc = jnp.split(proj, IN_SPLITS, axis=-1)
    ya = swa_sink_attention(qa, ka, va, swa_sinks, cos, sin)
    yb = s5_mixer(us, lam_re, lam_im, log_dt, b_re, b_im, c_re, c_im, d_skip, glu_w, glu_b)
    yc = fox_attention(qc, kc, vc, fc, fox_f_bias)
    ga, gb, gc = jnp.split(mix_gain, MIX_SPLITS, axis=-1)
    y = jnp.concatenate([rms_norm(ya, ga), rms_norm(yb, gb), rms_norm(yc, gc)], axis=-1)
    return y @ w_out

def setup_inputs(seed: int = 0) -> dict:
    key = jax.random.key(seed)
    ks = jax.random.split(key, 24)
    f32 = jnp.float32

    def nrm(k, shape, scale):
        return jax.random.normal(k, shape, f32) * scale

    x = nrm(ks[0], (BATCH, SEQ, D_MODEL), 1.0)
    norm_gains = 1.0 + nrm(ks[1], (DEPTH, 6, D_MODEL), 0.02)
    ffn1_gate = nrm(ks[2], (DEPTH, D_MODEL, D_FF), D_MODEL ** -0.5)
    ffn1_up = nrm(ks[3], (DEPTH, D_MODEL, D_FF), D_MODEL ** -0.5)
    ffn1_down = nrm(ks[4], (DEPTH, D_FF, D_MODEL), D_FF ** -0.5)
    w_in = nrm(ks[5], (DEPTH, D_MODEL, IN_WIDTH), D_MODEL ** -0.5)
    swa_sinks = nrm(ks[6], (DEPTH, SWA_Q_HEADS), 0.5)
    ssm_lambda_re = -0.5 + nrm(ks[7], (DEPTH, SSM_GROUPS, SSM_STATE), 0.01)
    ssm_lambda_im = (math.pi * jnp.arange(SSM_STATE, dtype=f32)
                     + nrm(ks[8], (DEPTH, SSM_GROUPS, SSM_STATE), 0.01))
    ssm_log_dt = jax.random.uniform(ks[9], (DEPTH, SSM_GROUPS), f32,
                                    math.log(SSM_DT_MIN), math.log(SSM_DT_MAX))
    ssm_b_re = nrm(ks[10], (DEPTH, SSM_GROUPS, SSM_STATE, SSM_GROUP_CH), (2 * SSM_GROUP_CH) ** -0.5)
    ssm_b_im = nrm(ks[11], (DEPTH, SSM_GROUPS, SSM_STATE, SSM_GROUP_CH), (2 * SSM_GROUP_CH) ** -0.5)
    ssm_c_re = nrm(ks[12], (DEPTH, SSM_GROUPS, SSM_GROUP_CH, SSM_STATE), (2 * SSM_STATE) ** -0.5)
    ssm_c_im = nrm(ks[13], (DEPTH, SSM_GROUPS, SSM_GROUP_CH, SSM_STATE), (2 * SSM_STATE) ** -0.5)
    ssm_d = nrm(ks[14], (DEPTH, SSM_WIDTH), 1.0)
    ssm_glu_w = nrm(ks[15], (DEPTH, SSM_WIDTH, SSM_WIDTH), SSM_WIDTH ** -0.5)
    ssm_glu_b = nrm(ks[16], (DEPTH, SSM_WIDTH), 0.01)
    fox_f_bias = jax.random.uniform(ks[17], (DEPTH, FOX_HEADS), f32, 1.0, 5.0)
    mix_norm_gain = 1.0 + nrm(ks[18], (DEPTH, MIX_WIDTH), 0.02)
    w_out = nrm(ks[19], (DEPTH, MIX_WIDTH, D_MODEL), MIX_WIDTH ** -0.5)
    ffn2_gate = nrm(ks[20], (DEPTH, D_MODEL, D_FF), D_MODEL ** -0.5)
    ffn2_up = nrm(ks[21], (DEPTH, D_MODEL, D_FF), D_MODEL ** -0.5)
    ffn2_down = nrm(ks[22], (DEPTH, D_FF, D_MODEL), D_FF ** -0.5)
    return {"x": x, "norm_gains": norm_gains, "ffn1_gate": ffn1_gate, "ffn1_up": ffn1_up,
            "ffn1_down": ffn1_down, "w_in": w_in, "swa_sinks": swa_sinks,
            "ssm_lambda_re": ssm_lambda_re, "ssm_lambda_im": ssm_lambda_im, "ssm_log_dt": ssm_log_dt,
            "ssm_b_re": ssm_b_re, "ssm_b_im": ssm_b_im, "ssm_c_re": ssm_c_re, "ssm_c_im": ssm_c_im,
            "ssm_d": ssm_d, "ssm_glu_w": ssm_glu_w, "ssm_glu_b": ssm_glu_b, "fox_f_bias": fox_f_bias,
            "mix_norm_gain": mix_norm_gain, "w_out": w_out, "ffn2_gate": ffn2_gate,
            "ffn2_up": ffn2_up, "ffn2_down": ffn2_down}

def reference(x, norm_gains, ffn1_gate, ffn1_up, ffn1_down, w_in, swa_sinks,
              ssm_lambda_re, ssm_lambda_im, ssm_log_dt, ssm_b_re, ssm_b_im, ssm_c_re, ssm_c_im,
              ssm_d, ssm_glu_w, ssm_glu_b, fox_f_bias, mix_norm_gain, w_out,
              ffn2_gate, ffn2_up, ffn2_down):
    cos, sin = rope_tables(x.shape[1])
    h = x
    for l in range(DEPTH):
        g = norm_gains[l]
        h = h + 0.5 * rms_norm(swiglu(rms_norm(h, g[0]), ffn1_gate[l], ffn1_up[l], ffn1_down[l]), g[1])
        m = hybrid_mixer(rms_norm(h, g[2]), w_in[l], swa_sinks[l], ssm_lambda_re[l], ssm_lambda_im[l],
                         ssm_log_dt[l], ssm_b_re[l], ssm_b_im[l], ssm_c_re[l], ssm_c_im[l], ssm_d[l],
                         ssm_glu_w[l], ssm_glu_b[l], fox_f_bias[l], mix_norm_gain[l], w_out[l], cos, sin)
        h = h + rms_norm(m, g[3])
        h = h + 0.5 * rms_norm(swiglu(rms_norm(h, g[4]), ffn2_gate[l], ffn2_up[l], ffn2_down[l]), g[5])
    return h


_drawn_inputs = setup_inputs


def setup_inputs(seed=0):
    import zlib

    import numpy as np

    out = dict(_drawn_inputs(seed))
    spreads = {}
    factors = {'swa_sinks': 8.0,
     'ssm_lambda_re': 8.0,
     'ssm_b_re': 2.68,
     'ssm_c_re': 2.684,
     'ssm_c_im': 2.671,
     'ssm_glu_b': 8.0,
     'mix_norm_gain': 2.872}
    for name, (base, spread) in spreads.items():
        noise = np.random.default_rng([zlib.crc32(name.encode()), seed]).standard_normal(out[name].shape)
        drawn = base * np.exp(spread * noise) if base else spread * noise
        out[name] = __import__('jax').numpy.asarray(drawn.astype(out[name].dtype))
    for name, factor in factors.items():
        out[name] = (out[name] * factor).astype(out[name].dtype)
    return out
```

```python
from contextlib import ExitStack

import numpy as np

import concourse.bass as bass
from concourse import mybir

F32 = mybir.dt.float32
F32R = mybir.dt.float32r
BF16 = mybir.dt.bfloat16
I32 = mybir.dt.int32
ALU = mybir.AluOpType
ACT = mybir.ActivationFunctionType
AX = mybir.AxisListType

P = 128
SEQ = 512
D_MODEL = 1024
DEPTH = 2
N_MLOAD = 3
D_FF = 2816
KD = D_MODEL // P
KF = D_FF // P
KH = KF // 2
TOK = SEQ // P
HD = 64
SWA_HEADS, FOX_HEADS = 8, 4
SWA_PAIRS, FOX_PAIRS = SWA_HEADS // 2, FOX_HEADS // 2
QA0, KA0, VA0, US0, QC0, KC0, VC0, FC0, IN_W = 0, 512, 640, 768, 1024, 1280, 1536, 1792, 1796
STATES = 64
ST = 16 * STATES // P
EPS = 1e-6
NEG = -1e30
SCALE = HD ** -0.5
TRAIL = 3
LAG_N, LAG_T, LAG_PV = 2, 3, 4
PROBS = 3
GELU_C = float(np.sqrt(2.0 / np.pi))

RAW_SLOTS, SPLIT_SLOTS = 4, 2
N_GU, N_DOWN, N_IN, N_OUT = 2 * KF, 2 * KD, 16, KD
U_GU1 = 0
U_DOWN1 = U_GU1 + N_GU
U_IN = U_DOWN1 + N_DOWN
U_OUT = U_IN + N_IN
U_GU2 = U_OUT + N_OUT
U_DOWN2 = U_GU2 + N_GU
U_LAYER = U_DOWN2 + N_DOWN
assert all(u % RAW_SLOTS == 0 for u in (U_DOWN1, U_IN, U_OUT, U_GU2, U_DOWN2, U_LAYER))

COLS = [("us0", US0), ("us1", US0 + P), ("fc", IN_W - P), ("ka", KA0), ("va", VA0),
        ("qa0", QA0), ("qa1", QA0 + P), ("qa2", QA0 + 2 * P), ("qa3", QA0 + 3 * P),
        ("kc0", KC0), ("vc0", VC0), ("qc0", QC0), ("kc1", KC0 + P), ("vc1", VC0 + P), ("qc1", QC0 + P)]
TILE = {name: m for m, (name, _) in enumerate(COLS)}
N_COLS = len(COLS)
N_AHEAD = TILE["kc0"]
PER_BANK = ((N_AHEAD + 1) // 2, N_COLS - (N_AHEAD + 1) // 2)
CUM0 = 96

ITEMS = [("swa", j, None, i, list(range(max(0, i - 1), i + 1))) for j in range(SWA_PAIRS) for i in range(TOK)]
ITEMS += [("fox", h // 2, h, i, list(range(i + 1))) for h in range(FOX_HEADS) for i in range(TOK)]
N_ITEMS = len(ITEMS)
N_PAIRS = SWA_PAIRS + FOX_PAIRS

def units_of(m):
    return (m, 1) if m < TILE["fc"] else (m, 2) if m == TILE["fc"] else (m + 1, 1)


def bank_of(m):
    return (m % 2, m // 2) if m < N_AHEAD else (1, N_AHEAD // 2 + m - N_AHEAD)


def last_item(pr):
    return (pr + 1) * TOK if pr < SWA_PAIRS else SWA_PAIRS * TOK + (pr - SWA_PAIRS + 1) * 2 * TOK


K_ID, K_CAUSAL, K_SWA, K_CMASK, K_COS, K_SIN = 0, 128, 256, 512, 640, 1152
K_ALL = 1664

R_GAIN, R_MIX, R_DSKIP, R_GLUB = 0, 96, 112, 116
R_A = 120
R_LRE, R_LIM, R_LDT = 0, 16, 32
R_B = 48


def constants():
    t = np.zeros((P, K_ALL), np.float32)
    q = np.arange(P)[:, None]
    k = np.arange(P)[None, :]
    t[:, K_ID:K_ID + P] = np.eye(P, dtype=np.float32)
    t[:, K_CAUSAL:K_CAUSAL + P] = np.where(k <= q, 0.0, NEG)
    t[:, K_SWA:K_SWA + P] = np.where((q < 64) & (k >= 64), 0.0, NEG)
    t[:, K_SWA + P:K_SWA + 2 * P] = np.where((q < 64) & (k >= 64), NEG, 0.0)
    t[:, K_CMASK:K_CMASK + P] = ((q // 16) % 2 == k // 64)
    inv = (np.float32(10000.0) ** (-np.arange(0, HD, 2, dtype=np.float32) / np.float32(HD))).astype(np.float32)
    ang = np.arange(SEQ, dtype=np.float32)[:, None] * inv[None, :]
    row = np.arange(P)
    t[:, K_COS:K_COS + SEQ] = np.cos(ang).T[row % 32]
    sign = np.where(row % 64 < 32, -1.0, 1.0).astype(np.float32)[:, None]
    t[:, K_SIN:K_SIN + SEQ] = np.sin(ang).T[row % 32] * sign
    return t


def build(nc, x, norm_gains, ffn1_gate, ffn1_up, ffn1_down, w_in, swa_sinks, lam_re, lam_im, log_dt,
          b_re, b_im, c_re, c_im, d_skip, glu_w, glu_b, fox_f_bias, mix_gain, w_out,
          ffn2_gate, ffn2_up, ffn2_down, const, out):
    tables = nc.dram_tensor("ssm_tables", (DEPTH * ST, P, 2, SEQ), F32, kind="Internal").ap()

    with ExitStack() as ctx:
        def sb(name, shape, dt=F32):
            return ctx.enter_context(nc.sbuf_tensor(name, shape, dt))

        def sem(name):
            return ctx.enter_context(nc.semaphore(name))

        hT = sb("hT", [P, KD, SEQ])
        xl = sb("xl", [P, KD, SEQ], F32R)
        with ExitStack() as alias:
            yF = alias.enter_context(nc.sbuf_tensor("yF", [P, KD, SEQ], F32))
        xh = sb("xh", [P, KD, SEQ], F32R)
        raw = sb("raw", [P, RAW_SLOTS, KH, P])
        wh = sb("wh", [P, SPLIT_SLOTS, KH, P], F32R)
        wl = sb("wl", [P, SPLIT_SLOTS, KH, P], F32R)
        sig = sb("sig", [P, 2, SEQ])
        full = sb("full", [P, 2, SEQ])
        sq = sb("sq", [P, 2, SEQ])
        acc = sb("acc", [P, SEQ])
        rstd = sb("rstd", [P, SEQ])
        prm = sb("prm", [P, R_A])
        ident = sb("ident", [P, P])
        identb = sb("identb", [P, P], BF16)
        maskb = sb("maskb", [P, K_CMASK - K_CAUSAL], BF16)
        ones = sb("ones", [P, P])
        eps_t = sb("eps_t", [P, 1])
        ln_t = sb("ln_t", [P, 1])
        sinks = sb("sinks", [P, DEPTH, SWA_HEADS])
        nsinks = sb("nsinks", [P, DEPTH, SWA_HEADS])
        fbias = sb("fbias", [P, DEPTH])
        ssm = sb("ssm", [P, 18, DEPTH * ST])
        tab1 = sb("tab1", [P, 2, ST, 32])
        tab32 = sb("tab32", [P, 2, ST, 16])
        tabw = sb("tabw", [P, 2, SEQ // 2])
        tabt = sb("tabt", [P, 2, SEQ // 2])
        wk = sb("wk", [P, 5, ST])
        stat = sb("stat", [P, PROBS, 8])

        with ExitStack() as inside:
            Hh = inside.enter_context(nc.sbuf_tensor("Hh", [P, KF, SEQ], F32R))
            Hl = inside.enter_context(nc.sbuf_tensor("Hl", [P, KF, SEQ], F32R))
        qa = sb("qa", [P, SWA_PAIRS, SEQ])
        qf = sb("qf", [P, FOX_HEADS, SEQ])
        us = sb("us", [P, 2, SEQ])
        with ExitStack() as alias:
            yM = alias.enter_context(nc.sbuf_tensor("yM", [P, KD, SEQ], F32))
        kz = sb("kz", [P, 4, SEQ])
        kf = sb("kf", [P, FOX_HEADS, SEQ])
        va = sb("va", [P, TOK, P])
        vc = sb("vc", [P, FOX_PAIRS, TOK, P])
        vT = sb("vT", [P, SEQ])
        cmask = sb("cmask", [P, P])
        cosr = sb("cosr", [P, 2, SEQ])
        tab = sb("tab", [P, 2, 2, SEQ])
        rot = sb("rot", [P, 4, SEQ])
        gst = sb("gst", [P, 2, SEQ])
        hst = sb("hst", [P, 2, SEQ])
        bT = sb("bT", [P, 2, 2, P])
        cT = sb("cT", [P, 2, 2, P])
        prob = sb("prob", [P, PROBS, SEQ])
        probT = sb("probT", [P, 2, SEQ])
        gluw = sb("gluw", [P, 2, 2 * P])
        bnat = prob[:, 0, 0:2 * P].rearrange("p (r t c) -> p r t c", r=2, t=ST)
        cnat = prob[:, 0, 2 * P:4 * P].rearrange("p (r t s) -> p r t s", r=2, t=2)
        bbd = prob[:, 1, :].rearrange("p (r t c) -> p r t c", r=2, t=ST)
        cbd = rot
        branch_r = [hst[:, 0, :], hst[:, 1, :], gst[:, 0, :]]

        ps = [ctx.enter_context(nc.psum_tensor(f"ps{b}", [P, SEQ], F32)) for b in range(8)]
        PROJ, S_BANK, PT_BANK, PV_BANK, Y_BANK = (0, 1), (2, 3), 4, 0, 5
        BU_BANK, POST_BANK, PRE_BANK = (6, 7), 6, 7
        DOWN, OUT = (4, 5), (2, 3)
        GLU_BANK = (5, 7)
        BRANCH = ((6, 0, 3, 4 * P), (5, 4, 5, 2 * P), (7, 6, 7, 2 * P))

        landed = [sem(f"weight_landed{i}") for i in range(RAW_SLOTS)]
        w_hi = sem("weight_hi_ready")
        w_split = sem("weight_split_ready")
        unit_done = sem("unit_multiplied")
        gu_free = sem("gate_up_banks_free")
        si_v = sem("silu_step_by_vector")
        si_a = sem("silu_step_by_scalar")
        h_full = sem("ffn_inside_ready")
        h_hi = sem("ffn_inside_hi_ready")
        h_lo = sem("ffn_inside_split_ready")
        sq_rdy = sem("square_of_output_ready")
        yv = sem("gained_output_ready")
        yn = sem("normed_output_ready")
        y_used = sem("output_bank_used")
        post_sum = sem("post_norm_sum_ready")
        post_r = sem("post_norm_rstd_ready")
        h_new = sem("residual_tile_ready")
        psq = sem("square_for_pre_norm_ready")
        pre_mm = sem("square_summed")
        pre_r = sem("pre_norm_rstd_ready")
        ln_rdy = sem("norm_logarithm_ready")
        x_full = sem("branch_tile_ready")
        x_hi = sem("input_tile_hi_ready")
        x_rdy = sem("input_tile_split_ready")
        dve_c = sem("vector_step")
        act_c = sem("scalar_step")
        pool_c = sem("pool_step")
        sp_gate = sem("sync_gate")
        pool_gate = sem("pool_gate")
        s_in = sem("params_landed")
        s_in2 = sem("input_rows_landed")
        s_small = sem("sinks_and_bias_landed")
        s_set = sem("params_spread")
        prm_rdy = sem("params_in_columns")
        s_set2 = sem("params_transposed")
        s_xt = sem("input_transposed")
        s_ssm = sem("ssm_scalars_ready")
        s_act0 = sem("ssm_function_done")
        tab_st = sem("table_stored")
        m_load = [sem(f"mixer_params_landed{i}") for i in range(2)]
        tab_ld = [sem(f"table_landed{i}") for i in range(2)]
        kz_zero = sem("padded_keys_cleared")
        bb_rdy = sem("block_diagonals_ready")
        bt_mm = sem("block_diagonals_transposed")
        bt_rdy = sem("ssm_matrices_ready")
        proj_free = [sem(f"projection_bank{i}_free") for i in range(2)]
        us_rdy = sem("ssm_input_ready")
        swp = sem("swapped_halves_ready")
        qk_rdy = sem("rotated_tile_ready")
        fox_rdy = sem("fox_q_or_k_ready")
        vt_rdy = sem("value_columns_ready")
        vt_mm = sem("values_transposed")
        v_rdy = sem("values_ready")
        f_x = sem("forget_logits_ready")
        f_e = sem("forget_exp_ready")
        f_ln = sem("forget_log_ready")
        cum_rdy = sem("forget_sum_ready")
        aug_ld = sem("forget_rows_landed")
        bu_free = sem("ssm_input_banks_free")
        bu_mm = sem("ssm_input_multiplied")
        rot_rdy = sem("ssm_products_ready")
        sc_rdy = sem("ssm_scanned")
        hs_rdy = sem("ssm_states_ready")
        sy_mm = sem("ssm_output_multiplied")
        s_mm = sem("scores_ready")
        s_max = sem("score_max_ready")
        s_exp = sem("score_exp_ready")
        s_prob = sem("probs_ready")
        pt_mm = sem("probs_transposed")
        pt_rdy = sem("probs_T_ready")
        pv_mm = sem("items_attended")
        o_free = sem("pair_output_ready")
        y0_rdy = sem("ssm_output_ready")
        gl_v = sem("glu_step_by_vector")
        gl_a = sem("glu_step_by_scalar")
        gl_lg = sem("glu_logits_ready")
        gl_mm = sem("glu_multiplied")
        br_ln = sem("branch_logarithm_ready")
        br_r = sem("branch_rstd_ready")
        s_row = sem("rows_transposed")
        s_rowc = sem("rows_copied")
        s_out = sem("output_stored")

        block = ctx.enter_context(nc.Block())

        def view2(t):
            return t.rearrange("p a b -> p (a b)")

        PRE = {"ffn1": (0, 0, 0), "mixer": (1, 1, 2), "ffn2": (2, 3, 4)}

        @block.sync
        def _(sp):
            sp.dma_start(yF[:, :, :].rearrange("p (t a) n -> p t (a n)", t=TOK),
                         x[0].rearrange("(t p) d -> p t d", p=P)).then_inc(s_in2, 16)
            sp.dma_start(ident[:, :], const[:, K_ID:K_ID + P]).then_inc(s_in, 16)
            sp.dma_start(sig[0:96, 0, 0:P], norm_gains.rearrange("l g (k p) -> (l g k) p", p=P)).then_inc(s_in, 16)
            sp.dma_start(sig[R_MIX:R_MIX + 16, 0, 0:P], mix_gain.rearrange("l (k p) -> (l k) p", p=P)).then_inc(s_in, 16)
            sp.dma_start(sig[R_DSKIP:R_DSKIP + 4, 0, 0:P], d_skip.rearrange("l (k p) -> (l k) p", p=P)).then_inc(s_in, 16)
            sp.dma_start(sig[R_GLUB:R_GLUB + 4, 0, 0:P], glu_b.rearrange("l (k p) -> (l k) p", p=P)).then_inc(s_in, 16)
            sp.dma_start(sig[R_LRE:R_LRE + 16, 1, 0:P],
                         lam_re.rearrange("l (t g) s -> (l t) (g s)", g=2)).then_inc(s_in, 16)
            sp.dma_start(sig[R_LIM:R_LIM + 16, 1, 0:P],
                         lam_im.rearrange("l (t g) s -> (l t) (g s)", g=2)).then_inc(s_in, 16)
            sp.dma_start(sig[R_LDT:R_LDT + 16, 1, P:P + 2],
                         log_dt.rearrange("l (t g) -> (l t) g", g=2)).then_inc(s_in, 16)
            sp.dma_start(full[:, 0, 0:K_CMASK - K_CAUSAL], const[:, K_CAUSAL:K_CMASK]).then_inc(s_in, 16)

            def load(n, slot, dst, src):
                sp.wait_ge(w_split, n + 1)
                sp.sem_inc(sp_gate, 1)
                sp.dma_start(dst, src).then_inc(landed[slot], 16)

            def columns(w, l, c0):
                return w[bass.ds(l, 1), :, c0].rearrange("a (k p) f -> p (a k) f", p=P)

            def ffn_loads(l, base_gu, base_down, gate, up, down):
                with sp.Fori(0, KF // 2) as j:
                    for i in range(4):
                        load(l * U_LAYER + j * 4 + base_gu + i, i, raw[:, i, 0:KD, :],
                             columns((gate, up)[i % 2], l, bass.ds(j * (2 * P) + (i // 2) * P, P)))
                with sp.Fori(0, KD // 2) as j:
                    for i in range(4):
                        rows = slice((i % 2) * KH * P, (i % 2 + 1) * KH * P)
                        load(l * U_LAYER + j * 4 + base_down + i, i, raw[:, i, :, :],
                             down[bass.ds(l, 1), rows, bass.ds(j * (2 * P) + (i // 2) * P, P)]
                             .rearrange("a (k p) f -> p (a k) f", p=P))

            with sp.Fori(0, DEPTH) as l:
                ffn_loads(l, U_GU1, U_DOWN1, ffn1_gate, ffn1_up, ffn1_down)
                for m, (_, c0) in enumerate(COLS):
                    u0, nu = units_of(m)
                    nk = KD // nu
                    for h in range(nu):
                        u = u0 + h
                        load(l * U_LAYER + U_IN + u, u % 4, raw[:, u % 4, 0:nk, :],
                             w_in[bass.ds(l, 1), h * nk * P:(h + 1) * nk * P, c0:c0 + P]
                             .rearrange("a (k p) f -> p (a k) f", p=P))
                with sp.Fori(0, N_OUT // 4) as j:
                    for i in range(4):
                        load(l * U_LAYER + j * 4 + U_OUT + i, i, raw[:, i, 0:KD, :],
                             columns(w_out, l, bass.ds(j * (4 * P) + i * P, P)))
                ffn_loads(l, U_GU2, U_DOWN2, ffn2_gate, ffn2_up, ffn2_down)
            for t in range(TOK):
                sp.wait_ge(s_rowc, TOK + t + 1)
                sp.dma_start(out[0, t * P:(t + 1) * P, :],
                             yF[:, 2 * t:2 * t + 2, :].rearrange("p a n -> p (a n)")).then_inc(s_out, 16)
            sp.wait_ge(s_out, 16 * TOK)

        @block.tensor
        def _(pe):
            pe.sem_inc(unit_done, SPLIT_SLOTS)
            pe.wait_ge(s_in, 16 * 9)
            pe.wait_ge(s_in2, 16)
            for k in range(KD):
                if k == 7:
                    pe.wait_ge(h_new, 1)
                for t in range(TOK):
                    mm = pe.transpose(ps[1 + k % 7][:, t * P:(t + 1) * P],
                                      yF[:, 2 * t + k // 4, (k % 4) * P:(k % 4 + 1) * P], ident[:, :])
                mm.then_inc(s_xt, 1)
                if k == 0:
                    pe.wait_ge(s_set, 1)
                    pe.transpose(ps[0][:, 0:R_A], sig[0:R_A, 0, 0:P], ident[0:R_A, 0:R_A]).then_inc(s_set2, 1)
                    pe.transpose(ps[0][:, P:P + R_B], sig[0:R_B, 1, 0:P], ident[0:R_B, 0:R_B]).then_inc(s_set2, 1)

            def three(bank, slot, kw, kx, first, last):
                pe.matmul(bank, wh[:, slot, kw, :], xh[:, kx, :], start=first, stop=False)
                pe.matmul(bank, wh[:, slot, kw, :], xl[:, kx, :], start=False, stop=False)
                return pe.matmul(bank, wl[:, slot, kw, :], xh[:, kx, :], start=False, stop=last)

            def unit_x(n, slot, bank, k0=0, nk=KD):
                pe.wait_ge(w_split, n + RAW_SLOTS + 1)
                for k in range(nk):
                    mm = three(bank, slot, k, k0 + k, k0 + k == 0, k0 + k == KD - 1)
                mm.then_inc(unit_done, 1)

            def first_two(n, banks, xn, ks, sums=None):
                def one(i, k):
                    if k == 0:
                        pe.wait_ge(w_split, n + i + RAW_SLOTS + 1)
                    mm = three(ps[banks[i]][:, :], i, k, k, k == 0, k == KD - 1)
                    if k == KD - 1:
                        mm.then_inc(unit_done, 1)

                for k in ks:
                    pe.wait_ge(x_rdy, xn * KD + k + 1)
                    one(0, k)
                    if k >= TRAIL:
                        one(1, k - TRAIL)
                    if sums is not None and k:
                        sums(k - 1)
                if ks[-1] == KD - 1:
                    if sums is not None:
                        sums(KD - 1)
                    for k in range(KD - TRAIL, KD):
                        one(1, k)

            def pre_sums(pn):
                def one(d):
                    pe.wait_ge(psq, pn * KD + d + 1)
                    pe.matmul(ps[PRE_BANK][:, :], ones[:, :], sq[:, d % 2, :],
                              start=(d == 0), stop=(d == KD - 1)).then_inc(pre_mm, 1)
                return one

            def post_norm(dn):
                pe.wait_ge(y_used, dn + KD + 2)
                pe.matmul(ps[POST_BANK][:, :], ones[:, :], acc[:, :], start=True, stop=True).then_inc(post_sum, 1)

            def ffn(l, base_gu, base_down, f_ffn, which, d_base):
                _, xi, _ = PRE[which]

                def pair(j, i0):
                    for i in range(i0, 4):
                        if i % 2 == 0:
                            pe.wait_ge(gu_free, l * (2 * KF) + j * 2 + f_ffn * KF + i // 2 + 1)
                        unit_x(l * U_LAYER + j * 4 + base_gu + i, i % 2, ps[i][:, :])

                pe.wait_ge(gu_free, l * (2 * KF) + f_ffn * KF + 1)
                first_two(l * U_LAYER + base_gu, (0, 1), l * 4 + xi, range(KD), pre_sums(l * 4 + xi))
                pair(0, 2)
                with pe.Fori(1, KF // 2) as j:
                    pair(j, 0)

                def down_pair(j, peeled):
                    for i in range(4):
                        n = l * U_LAYER + j * 4 + base_down + i
                        if i % 2 == 0:
                            pe.wait_ge(y_used, l * (3 * KD) + d_base + j * 2 + i // 2 + 1)
                        pe.wait_ge(w_split, n + RAW_SLOTS + 1)
                        if peeled and i < 2:
                            pe.wait_ge(h_lo, l * (2 * KF) + f_ffn * KF + (i + 1) * KH)
                        bank = ps[DOWN[i // 2]][:, :]
                        for k in range(KH):
                            f = (i % 2) * KH + k
                            pe.matmul(bank, wh[:, i % 2, k, :], Hh[:, f, :], start=(f == 0), stop=False)
                            pe.matmul(bank, wh[:, i % 2, k, :], Hl[:, f, :], start=False, stop=False)
                            mm = pe.matmul(bank, wl[:, i % 2, k, :], Hh[:, f, :], start=False, stop=(f == KF - 1))
                        mm.then_inc(unit_done, 1)

                down_pair(0, True)
                with pe.Fori(1, KD // 2) as j:
                    down_pair(j, False)
                post_norm(l * (3 * KD) + d_base)

            def mixer(l):
                base = l * U_LAYER + U_IN

                def project(m):
                    b, place = bank_of(m)
                    pe.wait_ge(proj_free[b], l * PER_BANK[b] + place + 1)
                    u0, nu = units_of(m)
                    for h in range(nu):
                        unit_x(base + u0 + h, (u0 + h) % 2, ps[PROJ[b]][:, :], h * (KD // nu), KD // nu)

                def project_half(m, half):
                    b, place = bank_of(m)
                    u = units_of(m)[0]
                    if half == 0:
                        pe.wait_ge(proj_free[b], l * PER_BANK[b] + place + 1)
                        pe.wait_ge(w_split, base + u + RAW_SLOTS + 1)
                    for k in range(half * (KD // 2), (half + 1) * (KD // 2)):
                        mm = three(ps[PROJ[b]][:, :], u % 2, k, k, k == 0, k == KD - 1)
                    if half:
                        mm.then_inc(unit_done, 1)

                def matrices():
                    pe.wait_ge(bb_rdy, l * 2 + 1)
                    for ri in range(2):
                        for T in range(2):
                            mm = pe.transpose(ps[2][:, (ri * 2 + T) * P:(ri * 2 + T + 1) * P],
                                              bbd[:, ri, 4 * T:4 * T + 4, :].rearrange("p a b -> p (a b)"), ident[:, :])
                    mm.then_inc(bt_mm, 1)
                    pe.wait_ge(bb_rdy, l * 2 + 2)
                    for ri in range(2):
                        for T in range(2):
                            mm = pe.transpose(ps[3][:, (ri * 2 + T) * P:(ri * 2 + T + 1) * P],
                                              cbd[:, ri * 2 + T, 0:P], ident[:, :])
                    mm.then_inc(bt_mm, 1)

                def values(v):
                    pe.wait_ge(vt_rdy, l * 3 + v + 1)
                    if v:
                        pe.wait_ge(pt_rdy, l * N_ITEMS + VALUES_AT[v] - LAG_T + 1)
                    for t in range(TOK):
                        mm = pe.transpose(ps[PT_BANK][:, t * P:(t + 1) * P], vT[:, t * P:(t + 1) * P], ident[:, :])
                    mm.then_inc(vt_mm, 1)

                def ssm_in(t):
                    pe.wait_ge(bu_free, l * ST + t + 1)
                    if t == 0:
                        pe.wait_ge(bt_rdy, l * 2 + 2)
                        pe.wait_ge(us_rdy, l * 2 + 2)
                    q = 32 * (t % 4)
                    for ri in range(2):
                        mm = pe.matmul(ps[BU_BANK[ri]][:, :], bT[q:q + 32, ri, t // 4, :], us[q:q + 32, t // 4, :],
                                       start=True, stop=True)
                    mm.then_inc(bu_mm, 1)

                def ssm_out(t):
                    pe.wait_ge(hs_rdy, l * ST + t + 1)
                    q = 32 * (t % 4)
                    bank = ps[Y_BANK]
                    if t == 4:
                        pe.wait_ge(y0_rdy, l * 2 + 1)
                    for ri in range(2):
                        mm = pe.matmul(bank[q:q + 32, :], cT[:, ri, t // 4, q:q + 32], hst[:, ri, :],
                                       start=(ri == 0), stop=(ri == 1), skip_group_check=True)
                    mm.then_inc(sy_mm, 1)

                def scores(n):
                    kind, j, h, i, keys = ITEMS[n]
                    g = l * N_ITEMS + n
                    if n >= 2:
                        pe.wait_ge(s_exp, g - 1)
                    bank = ps[S_BANK[n % 2]]
                    k0, nk = keys[0] * P, len(keys) * P
                    if kind == "swa":
                        if i == 0:
                            pe.wait_ge(qk_rdy, l * (1 + SWA_PAIRS) + 2 + j)
                        for a in range(2):
                            o = bank[:, a * 2 * P:a * 2 * P + nk]
                            pe.matmul(o, qa[:, j, i * P:(i + 1) * P], kz[:, 2 * (j // 2) + a, k0:k0 + nk],
                                      start=True, stop=False, skip_group_check=True)
                            mm = pe.matmul(o, identb[:, :], maskb[:, 3 * P - nk:3 * P],
                                           start=False, stop=True, skip_group_check=True)
                    else:
                        if i == 0 and h % 2 == 0:
                            pe.wait_ge(fox_rdy, l * 4 + 2 * (j + 1))
                            pe.wait_ge(aug_ld, (l + 1) * (2 * FOX_HEADS * 16))
                        pe.matmul(bank[:, 0:nk], qf[0:HD + 2, h, i * P:(i + 1) * P], kf[0:HD + 2, h, k0:k0 + nk],
                                  start=True, stop=False, skip_group_check=True)
                        mm = pe.matmul(bank[:, nk - P:nk], identb[:, :], maskb[:, 0:P],
                                       start=False, stop=True, skip_group_check=True)
                    mm.then_inc(s_mm, 1)

                def turn(n):
                    kind, j, h, i, keys = ITEMS[n]
                    g = l * N_ITEMS + n
                    pe.wait_ge(s_prob, g + 1)
                    if n:
                        pe.wait_ge(pt_rdy, g)
                    for v in range(3):
                        if n == (VALUES_AT[v] - LAG_T + 1 if v else 0):
                            pe.wait_ge(v_rdy, l * 3 + v + 1)
                    c = 0
                    for a in range(2 if kind == "swa" else 1):
                        for b in range(len(keys)):
                            mm = pe.transpose(ps[PT_BANK][:, c * P:(c + 1) * P],
                                              prob[:, n % PROBS, a * 2 * P + b * P:a * 2 * P + (b + 1) * P], ident[:, :])
                            c += 1
                    mm.then_inc(pt_mm, 1)

                def attend(n):
                    kind, j, h, i, keys = ITEMS[n]
                    g = l * N_ITEMS + n
                    pe.wait_ge(pt_rdy, g + 1)
                    pr = j if kind == "swa" else SWA_PAIRS + j
                    if n == 0:
                        pe.wait_ge(proj_free[0], l * PER_BANK[0] + PER_BANK[0] + 1)
                    if i == 0 and (kind == "swa" or h % 2 == 0) and pr:
                        pe.wait_ge(o_free, l * N_PAIRS + pr)
                    c = 0
                    for a in (range(2) if kind == "swa" else [h % 2]):
                        for b, kt in enumerate(keys):
                            if kind == "swa":
                                v = va[:, kt, (j // 2) * HD:(j // 2 + 1) * HD]
                            else:
                                v = vc[:, j, kt, a * HD:(a + 1) * HD]
                            mm = pe.matmul(ps[PV_BANK][64 * a:64 * a + 64, i * P:(i + 1) * P], v,
                                           probT[:, n % 2, c * P:(c + 1) * P], start=(b == 0),
                                           stop=(b == len(keys) - 1), skip_group_check=True)
                            c += 1
                    mm.then_inc(pv_mm, 1)

                def branch_sum(d):
                    pe.wait_ge(psq, (l * 4 + 2) * KD + d + 1)
                    bank, first, last, _ = [b for b in BRANCH if b[1] <= d <= b[2]][0]
                    if d == 0:
                        pe.wait_ge(bu_free, l * ST + ST + 1)
                    if d == 4:
                        pe.wait_ge(gl_lg, l * 2 + 1)
                    pe.matmul(ps[bank][:, :], ones[:, :], sq[:, d % 2, :], start=(d == first),
                              stop=(d == last)).then_inc(pre_mm, 1)

                def glu():
                    pe.wait_ge(gl_v, l * 6 + 4)
                    for m in range(2):
                        for k in range(2):
                            mm = pe.matmul(ps[GLU_BANK[m]][:, :], gluw[:, k, m * P:(m + 1) * P], us[:, k, :],
                                           start=(k == 0), stop=(k == 1))
                        mm.then_inc(gl_mm, 1)

                for m in range(2):
                    pe.wait_ge(proj_free[m], l * PER_BANK[m] + 1)
                first_two(base, PROJ, l * 4 + 1, range(KD), pre_sums(l * 4 + 1))
                matrices()
                for m in range(2, N_AHEAD):
                    project(m)
                    if m in SSM_IN_AHEAD:
                        ssm_in(SSM_IN_AHEAD[m])
                    if m in SSM_OUT_AHEAD:
                        ssm_out(SSM_OUT_AHEAD[m])
                    if m == TILE["va"] + 2:
                        values(0)
                for s in range(N_ITEMS + LAG_PV):
                    if s in SSM_OUT_AT:
                        ssm_out(SSM_OUT_AT[s])
                    if s in SSM_IN_AT:
                        ssm_in(SSM_IN_AT[s])
                    if s < N_ITEMS:
                        scores(s)
                    if s in PROJECT_AT:
                        project_half(PROJECT_AT[s], 0)
                    if s - 1 in PROJECT_AT:
                        project_half(PROJECT_AT[s - 1], 1)
                    if LAG_T <= s < N_ITEMS + LAG_T:
                        turn(s - LAG_T)
                    if s >= LAG_PV:
                        attend(s - LAG_PV)
                    if s in VALUES_AT:
                        values(VALUES_AT.index(s))
                    if s in SUM_AT:
                        branch_sum(SUM_AT[s])
                    if s == 19:
                        glu()
                n = l * U_LAYER + U_OUT
                pe.wait_ge(y_used, l * (3 * KD) + KD + 2)
                first_two(n, OUT, l * 4 + 2, range(0, 3))
                branch_sum(7)
                first_two(n, OUT, l * 4 + 2, range(3, KD))

                def out_four(j, i0):
                    for i in range(i0, 4):
                        pe.wait_ge(y_used, l * (3 * KD) + KD + j * 4 + i + 1)
                        unit_x(l * U_LAYER + j * 4 + U_OUT + i, i % 2, ps[OUT[i % 2]][:, :])

                out_four(0, 2)
                with pe.Fori(1, N_OUT // 4) as j:
                    out_four(j, 0)
                post_norm(l * (3 * KD) + KD)

            with pe.Fori(0, DEPTH) as l:
                ffn(l, U_GU1, U_DOWN1, 0, "ffn1", 0)
                mixer(l)
                ffn(l, U_GU2, U_DOWN2, 1, "ffn2", 2 * KD)
            for half in range(2):
                pe.wait_ge(h_new, KD + DEPTH * 3 * KD - (4 if half == 0 else 0))
                for t in range(TOK):
                    for k in range(4):
                        mm = pe.transpose(ps[2 * t + half][:, k * P:(k + 1) * P],
                                          hT[:, 4 * half + k, t * P:(t + 1) * P], ident[:, :])
                    mm.then_inc(s_row, 1)

        @block.scalar
        def _(act):
            for k in range(KD):
                act.wait_ge(s_xt, k + 1)
                act.activation(hT[:, k, :], ps[1 + k % 7][:, :], ACT.Copy).then_inc(h_new, 1)
            act.activation(maskb[:, :], full[:, 0, 0:K_CMASK - K_CAUSAL], ACT.Copy).then_inc(act_c, 1)
            act.activation(identb[:, :], ident[:, :], ACT.Copy).then_inc(act_c, 1)
            act.wait_ge(s_ssm, 1)
            act.activation(ssm[:, 3, :], ssm[:, 2, :], ACT.Exp).then_inc(s_act0, 1)
            act.wait_ge(s_ssm, 2)
            act.activation(ssm[:, 4, :], ssm[:, 4, :], ACT.Exp).then_inc(s_act0, 1)
            act.wait_ge(s_ssm, 3)
            act.activation(ssm[:, 8, :], ssm[:, 7, :], ACT.Sin).then_inc(s_act0, 1)
            act.activation(ssm[:, 9, :], ssm[:, 7, :], ACT.Sin, scale=0.5).then_inc(s_act0, 1)
            act.add_instruction(mybir.InstLoadActFuncSet(name=nc.get_next_instruction_name(),
                                                         act_func_set_id=EXP_LN_SET))
            act.activation(ln_t[:, :], eps_t[:, :], ACT.Ln).then_inc(act_c, 1)

            def split(n, q, slot4, slot2, nk):
                act.wait_ge(landed[slot4], q * 16 + 16)
                act.wait_ge(unit_done, n + 1)
                act.activation(wh[:, slot2, 0:nk, :], raw[:, slot4, 0:nk, :], ACT.Copy).then_inc(w_hi, 1)

            def split_first(l, base, i, nk=KD):
                split(l * U_LAYER + base + i, l * (U_LAYER // 4) + base // 4, i, i, nk)

            def root(total, width, r, lns, ln_count, done):
                act.activation(r, total, ACT.Ln, bias=eps_t[:, :], scale=1.0 / width).then_inc(lns, 1)
                act.wait_ge(lns, ln_count)
                act.activation(r, r, ACT.Exp, scale=-0.5).then_inc(done, 1)

            def post_norm(l, q, next_base=None):
                if next_base is not None:
                    split_first(l, next_base, 0)
                act.wait_ge(post_sum, l * 3 + q + 1)
                root(ps[POST_BANK][:, :], D_MODEL, rstd[:, :], ln_rdy, l * 6 + 2 * q + 2, post_r)

            def pre_norm(l, which, split_second, split_third):
                pi, xi, g = PRE[which]
                xn = l * 4 + xi
                for d in range(KD):
                    act.wait_ge(h_new, l * (3 * KD) + pi * KD + d + 1)
                    act.activation(xh[:, d, :], hT[:, d, :], ACT.Copy,
                                   scale=prm[:, bass.ds(l * 48 + g * KD + d, 1)]).then_inc(x_hi, 1)
                    if d >= 2:
                        act.wait_ge(pre_mm, xn * KD + d - 1)
                    act.activation(sq[:, d % 2, :], hT[:, d, :], ACT.Square).then_inc(psq, 1)
                    if d == 1:
                        split_second()
                split_third()
                act.wait_ge(pre_mm, xn * KD + KD)
                root(ps[PRE_BANK][:, :], D_MODEL, rstd[:, :], ln_rdy, l * 6 + 2 * pi + 1, pre_r)

            def square_out(dn, last_unit, bank):
                act.wait_ge(unit_done, last_unit + SPLIT_SLOTS + 1)
                act.wait_ge(y_used, dn + 1)
                act.activation(sq[:, bank % 2, :], ps[bank][:, :], ACT.Square).then_inc(sq_rdy, 1)

            def ffn(l, base_gu, base_down, f_ffn, d_base):
                def sigmoid(fn):
                    g, e = sig[:, 0, :], sig[:, 1, :]
                    act.wait_ge(si_v, fn * 4 + 1)
                    act.activation(e, g, ACT.Abs).then_inc(si_a, 1)
                    act.wait_ge(si_a, fn * 4 + 1)
                    act.activation(e, e, ACT.Exp, scale=-1.0).then_inc(si_a, 1)
                    act.wait_ge(si_a, fn * 4 + 2)
                    act.activation(e, e, ACT.Ln, bias=ones[:, 0:1]).then_inc(si_a, 1)
                    act.wait_ge(si_v, fn * 4 + 2)
                    act.activation(e, e, ACT.Exp).then_inc(si_a, 1)

                def high(fn, b, f_slice):
                    act.wait_ge(h_full, fn + 1)
                    act.activation(Hh[:, f_slice, :], full[:, b:b + 1, :], ACT.Copy).then_inc(h_hi, 1)

                def pair(j, i0):
                    for i in range(i0, 4):
                        if i0 == 0 or i == 3:
                            split(l * U_LAYER + j * 4 + base_gu + i, l * (U_LAYER // 4) + j + base_gu // 4, i, i % 2, KD)
                        f = j * 2 + i // 2 - 1
                        fn = l * (2 * KF) + f_ffn * KF + f
                        if i % 2 == 0:
                            sigmoid(fn)
                        else:
                            high(fn, 1 - i // 2, bass.ds(f, 1))

                pair(0, 2)
                with act.Fori(1, KF // 2) as j:
                    pair(j, 0)
                fn = l * (2 * KF) + f_ffn * KF + KF - 1

                def down_pair(j, peeled):
                    for i in range(4):
                        n = l * U_LAYER + j * 4 + base_down + i
                        split(n, l * (U_LAYER // 4) + j + base_down // 4, i, i % 2, KH)
                        if peeled and i == 0:
                            sigmoid(fn)
                            high(fn, 1, bass.ds(KF - 1, 1))
                        if i % 2 == 1 and not (peeled and i == 1):
                            square_out(l * (3 * KD) + d_base + j * 2 + i // 2 - 1, n - 2, DOWN[1 - i // 2])

                down_pair(0, True)
                with act.Fori(1, KD // 2) as j:
                    down_pair(j, False)
                square_out(l * (3 * KD) + d_base + KD - 1, l * U_LAYER + base_down + N_DOWN - 1, DOWN[1])

            def mixer(l):
                base = l * U_LAYER + U_IN

                def matrices():
                    act.wait_ge(bt_mm, l * 2 + 1)
                    act.activation(bT[:, :, :, :].rearrange("p a b c -> p (a b c)"), ps[2][:, :], ACT.Copy).then_inc(bt_rdy, 1)
                    act.wait_ge(bt_mm, l * 2 + 2)
                    act.activation(view2(cT[:, 0, :, :]), ps[3][:, 0:2 * P], ACT.Copy).then_inc(act_c, 1)
                    act.activation(view2(cT[:, 1, :, :]), ps[3][:, 2 * P:4 * P], ACT.Copy, scale=-1.0).then_inc(bt_rdy, 1)

                def swap(m, r):
                    act.wait_ge(unit_done, base + units_of(m)[0] + SPLIT_SLOTS + 1)
                    if r:
                        act.wait_ge(qk_rdy, l * (1 + SWA_PAIRS) + r)
                    for q in range(4):
                        o = 32 * (q ^ 1)
                        act.activation(sig[o:o + 32, 1, :], ps[PROJ[bank_of(m)[0]]][32 * q:32 * q + 32, :],
                                       ACT.Copy).then_inc(swp if q == 3 else act_c, 1)

                def values(v):
                    act.wait_ge(vt_mm, l * 3 + v + 1)
                    dst = va[:, :, :] if v == 0 else vc[:, v - 1, :, :]
                    act.activation(view2(dst), ps[PT_BANK][:, :], ACT.Copy).then_inc(v_rdy, 1)

                def forget():
                    r = slice(CUM0, P)
                    act.wait_ge(f_x, l + 1)
                    act.activation(full[r, 0, :], full[r, 1, :], ACT.Abs, bias=fbias[r, bass.ds(l, 1)]).then_inc(f_e, 1)
                    act.wait_ge(f_e, l * 2 + 1)
                    act.activation(full[r, 0, :], full[r, 0, :], ACT.Exp, scale=-1.0).then_inc(f_e, 1)
                    act.wait_ge(f_e, l * 2 + 2)
                    act.activation(full[r, 0, :], full[r, 0, :], ACT.Ln, bias=ones[r, 0:1]).then_inc(f_ln, 1)

                def split_unit(u):
                    split(base + u, l * (U_LAYER // 4) + (U_IN + u) // 4, u % 4, u % 2,
                          KD // 2 if units_of(TILE["fc"])[0] in (u, u - 1) else KD)

                rotated = 0
                for u in range(2, N_AHEAD + 3):
                    if u > 2:
                        split_unit(u)
                    if u == 2:
                        matrices()
                    m = u - 3
                    if m == TILE["fc"]:
                        pass
                    elif m > TILE["fc"] and COLS[m][0][:2] in ("ka", "qa"):
                        swap(m, rotated)
                        rotated += 1
                    if m == TILE["fc"] + 1:
                        forget()
                    if m == TILE["va"] + 3:
                        values(0)

                def exps(n):
                    kind, j, h, i, keys = ITEMS[n]
                    act.wait_ge(s_max, l * N_ITEMS + n + 1)
                    nk = len(keys) * P
                    b = n % PROBS
                    if kind == "swa":
                        for a in range(2):
                            act.activation(prob[:, b, a * 2 * P:a * 2 * P + nk],
                                           ps[S_BANK[n % 2]][:, a * 2 * P:a * 2 * P + nk], ACT.Exp,
                                           bias=stat[:, b, a:a + 1],
                                           accum_out=stat[:, b, 2 + a:3 + a]).then_inc(act_c, 1)
                        for a in range(2):
                            act.activation(stat[:, b, 4 + a:5 + a],
                                           sinks[:, bass.ds(l, 1), 2 * j + a:2 * j + a + 1].rearrange("p a h -> p (a h)"),
                                           ACT.Exp, bias=stat[:, b, a:a + 1]).then_inc(s_exp if a else act_c, 1)
                    else:
                        act.activation(prob[:, b, 0:nk], ps[S_BANK[n % 2]][:, 0:nk], ACT.Exp,
                                       bias=stat[:, b, 0:1], accum_out=stat[:, b, 2:3]).then_inc(s_exp, 1)

                def turned(n):
                    kind, j, h, i, keys = ITEMS[n]
                    g = l * N_ITEMS + n
                    act.wait_ge(pt_mm, g + 1)
                    if n >= 2:
                        act.wait_ge(pv_mm, g - 1)
                    w = len(keys) * P * (2 if kind == "swa" else 1)
                    act.activation(probT[:, n % 2, 0:w], ps[PT_BANK][:, 0:w], ACT.Copy).then_inc(pt_rdy, 1)

                def pair_out(pr):
                    act.wait_ge(pv_mm, l * N_ITEMS + last_item(pr))
                    dst = qa[:, pr, :] if pr < SWA_PAIRS else qf[:, 2 * (pr - SWA_PAIRS), :]
                    act.activation(dst, ps[PV_BANK][:, :], ACT.Copy).then_inc(o_free, 1)

                def square(d):
                    if d < 4:
                        src = qa[:, d, :]
                        act.wait_ge(o_free, l * N_PAIRS + d + 1)
                    elif d < 6:
                        src = us[:, d - 4, :]
                        act.wait_ge(gl_v, l * 6 + d + 1)
                    else:
                        src = qf[:, 2 * (d - 6), :]
                        act.wait_ge(o_free, l * N_PAIRS + d - 1)
                    if d >= 2:
                        act.wait_ge(pre_mm, (l * 4 + 2) * KD + d - 1)
                    act.activation(sq[:, d % 2, :], src, ACT.Square).then_inc(psq, 1)

                def sigmoid_of(z, c, done):
                    act.activation(z, z, ACT.Exp, scale=-c).then_inc(gl_a, 1)
                    act.wait_ge(gl_a, done + 1)
                    act.activation(z, z, ACT.Ln, bias=ones[:, 0:1]).then_inc(gl_a, 1)
                    act.wait_ge(gl_a, done + 2)
                    act.activation(z, z, ACT.Exp, scale=-1.0).then_inc(gl_a, 1)

                def branch_root(b):
                    bank, _, last, width = BRANCH[b]
                    act.wait_ge(pre_mm, (l * 4 + 2) * KD + last + 1)
                    if b == 0:
                        act.wait_ge(sy_mm, l * ST + ST)
                    root(ps[bank][:, :], width, branch_r[b], br_ln, l * 3 + b + 1, br_r)

                def x_high(d):
                    act.wait_ge(x_full, l * KD + d + 1)
                    act.activation(xh[:, d, :], full[:, d % 2, :], ACT.Copy).then_inc(x_hi, 1)

                for s in range(N_ITEMS + LAG_PV):
                    if LAG_T <= s < N_ITEMS + LAG_T:
                        turned(s - LAG_T)
                    if s < N_ITEMS:
                        exps(s)
                    for pr in range(N_PAIRS):
                        if s == last_item(pr) + LAG_PV - 1:
                            pair_out(pr)
                    if s in VALUES_AT:
                        values(VALUES_AT.index(s))
                    if s - 2 in PROJECT_AT and PROJECT_AT[s - 2] + 2 < N_COLS:
                        split_unit(units_of(PROJECT_AT[s - 2] + 2)[0])
                    if s in SQUARE_AT:
                        square(SQUARE_AT[s])
                    if s - 1 in GELU_AT:
                        T = GELU_AT.index(s - 1)
                        act.wait_ge(gl_v, l * 6 + 2 * T + 1)
                        sigmoid_of(sig[:, 1, :], 2.0 * GELU_C, l * 12 + 3 * T)
                    if s in (20, 21):
                        m = s - 20
                        act.wait_ge(gl_lg, l * 2 + m + 1)
                        sigmoid_of(gst[:, m, :], 1.0, l * 12 + 6 + 3 * m)
                    if s == 22:
                        branch_root(0)
                    if s == 27:
                        branch_root(1)
                    if s in XHI_AT:
                        x_high(XHI_AT[s])
                    if s == 30:
                        split_first(l, U_OUT, 0)
                        split_first(l, U_OUT, 1)
                square(7)
                branch_root(2)
                x_high(6)
                x_high(7)

                def out_four(j, i0):
                    for i in range(i0, 4):
                        n = l * U_LAYER + j * 4 + U_OUT + i
                        split(n, l * (U_LAYER // 4) + j + U_OUT // 4, i, i % 2, KD)
                        square_out(l * (3 * KD) + KD + j * 4 + i - 2, n - 2, OUT[i % 2])

                out_four(0, 2)
                with act.Fori(1, N_OUT // 4) as j:
                    out_four(j, 0)
                for i in (2, 3):
                    square_out(l * (3 * KD) + KD + 4 + i, l * U_LAYER + U_OUT + 4 + i, OUT[i % 2])

            act.wait_ge(prm_rdy, 1)
            with act.Fori(0, DEPTH) as l:
                split_first(l, U_GU1, 0)
                pre_norm(l, "ffn1", lambda: split_first(l, U_GU1, 1),
                         lambda: split(l * U_LAYER + U_GU1 + 2, l * (U_LAYER // 4) + U_GU1 // 4, 2, 0, KD))
                ffn(l, U_GU1, U_DOWN1, 0, 0)
                post_norm(l, 0, U_IN)
                pre_norm(l, "mixer", lambda: split_first(l, U_IN, 1),
                         lambda: split(l * U_LAYER + U_IN + 2, l * (U_LAYER // 4) + U_IN // 4, 2, 0, KD // 2))
                mixer(l)
                post_norm(l, 1, U_GU2)
                pre_norm(l, "ffn2", lambda: split_first(l, U_GU2, 1),
                         lambda: split(l * U_LAYER + U_GU2 + 2, l * (U_LAYER // 4) + U_GU2 // 4, 2, 0, KD))
                ffn(l, U_GU2, U_DOWN2, 1, 2 * KD)
                post_norm(l, 2)
            for half in range(2):
                for t in range(TOK):
                    act.wait_ge(s_row, half * TOK + t + 1)
                    if half == 0 and t == 0:
                        act.wait_ge(h_new, KD + DEPTH * 3 * KD)
                    act.activation(yF[:, 2 * t + half, :], ps[2 * t + half][:, :], ACT.Copy).then_inc(s_rowc, 1)

        @block.vector
        def _(dve):
            V = nc.vector
            steps = [0]

            def link(ins):
                steps[0] += 1
                ins.then_inc(dve_c, 1)
                dve.wait_ge(dve_c, steps[0])

            dve.sem_inc(w_split, RAW_SLOTS)
            dve.sem_inc(gu_free, 2)
            dve.sem_inc(y_used, 2)
            dve.sem_inc(bu_free, 1)
            dve.sem_inc(proj_free[0], 1)
            dve.sem_inc(proj_free[1], 1)
            V.memset(ones[:, :], 1.0).then_inc(dve_c, 1)
            V.memset(eps_t[:, :], EPS).then_inc(dve_c, 1)
            steps[0] += 2
            dve.wait_ge(s_in, 16 * 9)
            link(V.tensor_copy(sig[R_LDT:R_LDT + 16, 1, 0:P].rearrange("p (g s) -> p g s", g=2),
                               sig[R_LDT:R_LDT + 16, 1, P:P + 2].unsqueeze(2).to_broadcast([16, 2, STATES])))
            dve.sem_inc(s_set, 1)
            dve.wait_ge(s_set2, 2)
            link(V.tensor_copy(prm[:, :], ps[0][:, 0:R_A]))
            dve.sem_inc(prm_rdy, 1)
            (LR, LI, LDT, DT, MAG, TH, KK, RR, SN, SH, CS, ABR, ABI, T1, T2, DEN, ZR, ZI) = range(18)

            def s(i):
                return ssm[:, i, :]

            def tt(o, a, b, op):
                link(V.tensor_tensor(s(o), s(a), s(b), op))

            link(V.tensor_scalar(s(LR), ps[0][:, P + R_LRE:P + R_LRE + 16], -1e-4, None, ALU.min))
            link(V.tensor_copy(s(LI), ps[0][:, P + R_LIM:P + R_LIM + 16]))
            link(V.tensor_copy(s(LDT), ps[0][:, P + R_LDT:P + R_LDT + 16]))
            dve.sem_inc(s_ssm, 1)
            dve.wait_ge(s_small, 32)
            link(V.tensor_scalar(nsinks[:, :, :], sinks[:, :, :], -1.0, None, ALU.mult))
            dve.wait_ge(s_act0, 1)
            tt(MAG, LR, DT, ALU.mult)
            dve.sem_inc(s_ssm, 1)
            tt(TH, LI, DT, ALU.mult)
            link(V.tensor_scalar(s(KK).bitcast(I32), s(TH), 1.0 / (2 * np.pi), None, ALU.mult))
            link(V.tensor_copy(s(T1), s(KK).bitcast(I32)))
            C1 = 6.28125
            C2 = float(np.round((2 * np.pi - C1) * 2.0 ** 20) / 2.0 ** 20)
            C3 = float(2 * np.pi - C1 - C2)
            for c in (C1, C2, C3):
                link(V.scalar_tensor_tensor(s(TH), s(T1), -c, s(TH), ALU.mult, ALU.add))
            PI = float(np.nextafter(np.float32(np.pi), np.float32(0)))
            link(V.tensor_scalar(s(RR), s(TH), PI, -PI, ALU.min, ALU.max))
            dve.sem_inc(s_ssm, 1)
            dve.wait_ge(s_act0, 4)
            tt(T1, SH, SH, ALU.mult)
            link(V.tensor_scalar(s(CS), s(T1), -2.0, 1.0, ALU.mult, ALU.add))
            tt(ABR, MAG, CS, ALU.mult)
            tt(ABI, MAG, SN, ALU.mult)
            link(V.tensor_scalar(s(ABR), s(ABR), -1.0, None, ALU.add))
            tt(T1, LR, LR, ALU.mult)
            tt(T2, LI, LI, ALU.mult)
            tt(DEN, T1, T2, ALU.add)
            link(V.reciprocal(s(DEN), s(DEN)))
            tt(T1, ABR, LR, ALU.mult)
            tt(T2, ABI, LI, ALU.mult)
            tt(T1, T1, T2, ALU.add)
            tt(ZR, T1, DEN, ALU.mult)
            tt(T1, ABI, LR, ALU.mult)
            tt(T2, ABR, LI, ALU.mult)
            tt(T1, T1, T2, ALU.subtract)
            tt(ZI, T1, DEN, ALU.mult)
            dve.sem_inc(s_ssm, 1)
            setup = steps[0]

            def low(n, slot4, slot2, nk):
                dve.wait_ge(w_hi, n + 1)
                V.tensor_tensor(wl[:, slot2, 0:nk, :], raw[:, slot4, 0:nk, :],
                                wh[:, slot2, 0:nk, :].bitcast(F32), ALU.subtract).then_inc(w_split, 1)

            def low_first(l, base, i):
                low(l * U_LAYER + base + i, i, i, KD)

            def x_low(l, which, d):
                _, xi, g = PRE[which]
                dve.wait_ge(x_hi, (l * 4 + xi) * KD + d + 1)
                V.scalar_tensor_tensor(xl[:, d, :], hT[:, d, :], prm[:, bass.ds(l * 48 + g * KD + d, 1)],
                                       xh[:, d, :].bitcast(F32), ALU.mult, ALU.subtract).then_inc(x_rdy, 1)

            def out_tile(l, dn, y, d, half, bank, which, first):
                dve.wait_ge(sq_rdy, dn + 1)
                V.tensor_scalar(y, ps[bank][:, :], prm[:, bass.ds(l * 48 + which * KD + d, 1)], half,
                                ALU.mult, ALU.mult).then_inc(yv, 1)
                if first:
                    V.tensor_copy(acc[:, :], sq[:, bank % 2, :]).then_inc(y_used, 1)
                else:
                    dve.wait_ge(y_used, dn + 2)
                    V.tensor_tensor(acc[:, :], acc[:, :], sq[:, bank % 2, :], ALU.add).then_inc(y_used, 1)

            def post_norm(l, q, y, next_which=None, next_base=None):
                qn = l * 3 + q
                if next_base is not None:
                    low_first(l, next_base, 0)
                dve.wait_ge(yv, qn * KD + KD)
                dve.wait_ge(post_r, qn + 1)
                for d in range(KD + 2):
                    if d < KD:
                        V.tensor_tensor(y(d), y(d), rstd[:, :], ALU.mult).then_inc(yn, 1)
                    if 1 <= d <= KD:
                        dve.wait_ge(yn, qn * KD + d)
                        V.tensor_tensor(hT[:, d - 1, :], hT[:, d - 1, :], y(d - 1), ALU.add).then_inc(h_new, 1)
                    if d == 4 and next_base is not None:
                        low_first(l, next_base, 1)
                    if d >= 2 and next_which is not None:
                        x_low(l, next_which, d - 2)

            def ffn(l, base_gu, base_down, f_ffn, d_base, post_gain):
                def silu(fn, b, between):
                    g, e = sig[:, 0, :], sig[:, 1, :]
                    V.tensor_tensor(g, ps[2 * b][:, :], rstd[:, :], ALU.mult).then_inc(si_v, 1)
                    between()
                    dve.wait_ge(si_a, fn * 4 + 3)
                    V.scalar_tensor_tensor(e, g, 0.0, e, ALU.min, ALU.subtract).then_inc(si_v, 1)
                    dve.wait_ge(si_a, fn * 4 + 4)
                    V.tensor_tensor(e, g, e, ALU.mult).then_inc(si_v, 1)
                    dve.wait_ge(si_v, fn * 4 + 3)
                    V.tensor_tensor(e, e, rstd[:, :], ALU.mult).then_inc(si_v, 1)

                def times_up(fn, b, n_up):
                    dve.wait_ge(unit_done, n_up + SPLIT_SLOTS + 1)
                    dve.wait_ge(si_v, fn * 4 + 4)
                    V.tensor_tensor(full[:, b, :], ps[2 * b + 1][:, :], sig[:, 1, :], ALU.mult).then_inc(h_full, 1)
                    dve.wait_ge(h_full, fn + 1)
                    dve.sem_inc(gu_free, 1)

                def low_h(fn, b, f_slice):
                    dve.wait_ge(h_hi, fn + 1)
                    V.tensor_tensor(Hl[:, f_slice, :], full[:, b:b + 1, :], Hh[:, f_slice, :].bitcast(F32),
                                    ALU.subtract).then_inc(h_lo, 1)

                def pair(j, i0, first_f=False):
                    for i in range(i0, 4):
                        n = l * U_LAYER + j * 4 + base_gu + i
                        if i0 == 0 or i == 3:
                            low(n, i, i % 2, KD)
                        f = j * 2 + i // 2 - 1
                        fn = l * (2 * KF) + f_ffn * KF + f
                        b = 1 - i // 2
                        if i % 2 == 0:
                            dve.wait_ge(unit_done, n - 2 + SPLIT_SLOTS + 1)
                            silu(fn, b, (lambda: None) if first_f else
                                 (lambda: low_h(fn - 1, 1 - b, bass.ds(f - 1, 1))))
                        else:
                            times_up(fn, b, n - 2)

                low(l * U_LAYER + base_gu + 2, 2, 0, KD)
                dve.wait_ge(pre_r, l * 3 + (0 if f_ffn == 0 else 2) + 1)
                pair(0, 2, True)
                with dve.Fori(1, KF // 2) as j:
                    pair(j, 0)
                fn = l * (2 * KF) + f_ffn * KF + KF - 1

                def down_pair(j, peeled):
                    for i in range(4):
                        n = l * U_LAYER + j * 4 + base_down + i
                        low(n, i, i % 2, KH)
                        if peeled and i == 0:
                            dve.wait_ge(unit_done, l * U_LAYER + base_gu + N_GU - 2 + SPLIT_SLOTS + 1)
                            silu(fn, 1, lambda: low_h(fn - 1, 0, bass.ds(KF - 2, 1)))
                            times_up(fn, 1, l * U_LAYER + base_gu + N_GU - 1)
                            low_h(fn, 1, bass.ds(KF - 1, 1))
                        if i % 2 == 1 and not (peeled and i == 1):
                            d = j * 2 + i // 2 - 1
                            out_tile(l, l * (3 * KD) + d_base + d,
                                     yF[:, bass.ds(d, 1), :].rearrange("p a n -> p (a n)"), d, 0.5,
                                     DOWN[1 - i // 2], post_gain, peeled)

                down_pair(0, True)
                with dve.Fori(1, KD // 2) as j:
                    down_pair(j, False)
                out_tile(l, l * (3 * KD) + d_base + KD - 1, yF[:, KD - 1, :], KD - 1, 0.5, DOWN[1], post_gain, False)

            def mixer(l):
                base = l * U_LAYER + U_IN
                mstep = [0]

                def mlink(ins):
                    mstep[0] += 1
                    ins.then_inc(dve_c, 1)
                    dve.wait_ge(dve_c, l * M_STEPS + setup + mstep[0])

                def complete(m):
                    u0, nu = units_of(m)
                    dve.wait_ge(unit_done, base + u0 + nu - 1 + SPLIT_SLOTS + 1)

                def free(m, done, count):
                    dve.wait_ge(done, count)
                    dve.sem_inc(proj_free[bank_of(m)[0]], 1)

                def rotate(m, r, scale, outs):
                    dve.wait_ge(swp, l * (1 + SWA_PAIRS) + r + 1)
                    mlink(V.scalar_tensor_tensor(sig[:, 0, :], ps[PROJ[bank_of(m)[0]]][:, :], scale, cosr[:, 0, :],
                                                 ALU.mult, ALU.mult))
                    dve.sem_inc(proj_free[bank_of(m)[0]], 1)
                    mlink(V.scalar_tensor_tensor(sig[:, 1, :], sig[:, 1, :], scale, cosr[:, 1, :], ALU.mult, ALU.mult))
                    for dst, rows in outs[:-1]:
                        V.tensor_tensor(dst, sig[rows, 0, :], sig[rows, 1, :], ALU.add).then_inc(dve_c, 1)
                        mstep[0] += 1
                    dst, rows = outs[-1]
                    V.tensor_tensor(dst, sig[rows, 0, :], sig[rows, 1, :], ALU.add).then_inc(qk_rdy, 1)

                def ssm_input(m):
                    complete(m)
                    V.tensor_tensor(us[:, m, :], ps[PROJ[bank_of(m)[0]]][:, :], rstd[:, :], ALU.mult).then_inc(us_rdy, 1)
                    free(m, us_rdy, l * 2 + m + 1)

                def value_columns(m, v):
                    complete(m)
                    if v:
                        dve.wait_ge(vt_mm, l * 3 + v)
                    V.tensor_tensor(vT[:, :], ps[PROJ[bank_of(m)[0]]][:, :], rstd[:, :], ALU.mult).then_inc(vt_rdy, 1)
                    free(m, vt_rdy, l * 3 + v + 1)

                def fox_tile(m, order):
                    complete(m)
                    name = COLS[m][0]
                    dst, scale = (qf, SCALE) if name[0] == "q" else (kf, 1.0)
                    for a in range(2):
                        rows = slice(HD * a, HD * a + HD)
                        V.scalar_tensor_tensor(dst[0:HD, 2 * int(name[2]) + a, :], ps[PROJ[bank_of(m)[0]]][rows, :], scale,
                                               rstd[rows, :], ALU.mult, ALU.mult).then_inc(fox_rdy if a else dve_c, 1)
                    mstep[0] += 1
                    free(m, fox_rdy, l * 4 + order + 1)

                def forget(m):
                    r = slice(CUM0, P)
                    complete(m)
                    mlink(V.tensor_tensor(full[r, 1, :], ps[PROJ[bank_of(m)[0]]][r, :], rstd[r, :], ALU.mult))
                    dve.sem_inc(proj_free[bank_of(m)[0]], 1)
                    dve.sem_inc(f_x, 1)

                def forget_sum():
                    r = slice(CUM0, P)
                    dve.wait_ge(f_ln, l + 1)
                    mlink(V.tensor_scalar(full[r, 1, :], full[r, 1, :], fbias[r, bass.ds(l, 1)], 0.0,
                                          ALU.add, ALU.min))
                    mlink(V.tensor_tensor(full[r, 1, :], full[r, 1, :], full[r, 0, :], ALU.subtract))
                    mlink(V.tensor_tensor_scan(full[r, 0, :], ones[r, 0:1].to_broadcast([32, SEQ]), full[r, 1, :], 0.0,
                                               ALU.mult, ALU.add))
                    mlink(V.tensor_scalar(full[r, 1, :], full[r, 0, :], -1.0, None, ALU.mult))
                    dve.sem_inc(cum_rdy, 1)

                def ssm_turn(t):
                    g = l * ST + t
                    dve.wait_ge(bu_mm, g + 1)
                    dve.wait_ge(tab_ld[t % 2], l * (8 * ST) + (t // 2 + 1) * 16)
                    if t:
                        dve.wait_ge(sc_rdy, g * 2)
                    C, S = tab[:, t % 2, 0, :], tab[:, t % 2, 1, :]
                    for o, (b, c) in enumerate(((0, C), (1, S), (1, C), (0, S))):
                        V.tensor_tensor(rot[:, o, :], ps[BU_BANK[b]][:, :], c, ALU.mult).then_inc(rot_rdy, 1)
                    dve.wait_ge(rot_rdy, g * 6 + 4)
                    dve.sem_inc(bu_free, 1)
                    V.tensor_tensor(rot[:, 0, :], rot[:, 0, :], rot[:, 1, :], ALU.add).then_inc(rot_rdy, 1)
                    V.tensor_tensor(rot[:, 2, :], rot[:, 2, :], rot[:, 3, :], ALU.subtract).then_inc(rot_rdy, 1)

                def ssm_scan(t):
                    g = l * ST + t
                    dve.wait_ge(rot_rdy, g * 6 + 6)
                    if t:
                        dve.wait_ge(hs_rdy, g)
                    for ri in range(2):
                        V.tensor_tensor_scan(gst[:, ri, :], ssm[:, MAG, bass.ds(l * ST + t, 1)].to_broadcast([P, SEQ]),
                                             rot[:, 2 * ri, :], 0.0, ALU.mult, ALU.add).then_inc(sc_rdy, 1)

                def skip(T):
                    dve.wait_ge(sy_mm, l * ST + 4 * T + 4)
                    V.scalar_tensor_tensor(us[:, T, :], us[:, T, :], prm[:, bass.ds(R_DSKIP + l * 2 + T, 1)],
                                           ps[Y_BANK][:, :], ALU.mult, ALU.add).then_inc(y0_rdy, 1)

                def maxes(n):
                    kind, j, h, i, keys = ITEMS[n]
                    b = n % PROBS
                    nk = len(keys) * P
                    dve.wait_ge(s_mm, l * N_ITEMS + n + 1)
                    if kind == "swa":
                        mlink(V.tensor_reduce(stat[:, b, 0:2],
                                              ps[S_BANK[n % 2]][:, :].rearrange("p (a k) -> p a k", a=2)[:, :, 0:nk],
                                              AX.X, ALU.max, negate=True))
                        V.tensor_tensor(stat[:, b, 0:2], stat[:, b, 0:2],
                                        nsinks[:, bass.ds(l, 1), 2 * j:2 * j + 2].rearrange("p a h -> p (a h)"),
                                        ALU.min).then_inc(s_max, 1)
                    else:
                        V.tensor_reduce(stat[:, b, 0:1], ps[S_BANK[n % 2]][:, 0:nk], AX.X, ALU.max,
                                        negate=True).then_inc(s_max, 1)

                def norms(n):
                    kind, j, h, i, keys = ITEMS[n]
                    b = n % PROBS
                    nk = len(keys) * P
                    dve.wait_ge(s_exp, l * N_ITEMS + n + 1)
                    if kind == "swa":
                        mlink(V.tensor_tensor(stat[:, b, 2:4], stat[:, b, 2:4], stat[:, b, 4:6], ALU.add))
                        mlink(V.reciprocal(stat[:, b, 2:4], stat[:, b, 2:4]))
                        V.tensor_scalar(prob[:, b, 0:nk], prob[:, b, 0:nk], stat[:, b, 2:3], None,
                                        ALU.mult).then_inc(dve_c, 1)
                        mstep[0] += 1
                        V.tensor_scalar(prob[:, b, 2 * P:2 * P + nk], prob[:, b, 2 * P:2 * P + nk],
                                        stat[:, b, 3:4], None, ALU.mult).then_inc(s_prob, 1)
                    else:
                        mlink(V.reciprocal(stat[:, b, 2:3], stat[:, b, 2:3]))
                        V.tensor_scalar(prob[:, b, 0:nk], prob[:, b, 0:nk], stat[:, b, 2:3], None,
                                        ALU.mult).then_inc(s_prob, 1)

                def x_tile(d):
                    b = 0 if d < 4 else 1 if d < 6 else 2
                    src = qa[:, d, :] if d < 4 else us[:, d - 4, :] if d < 6 else qf[:, 2 * (d - 6), :]
                    dve.wait_ge(br_r, l * 3 + b + 1)
                    if d >= 2:
                        dve.wait_ge(x_rdy, (l * 4 + 2) * KD + d - 1)
                    V.scalar_tensor_tensor(full[:, d % 2, :], src, prm[:, bass.ds(R_MIX + l * 8 + d, 1)],
                                           branch_r[b], ALU.mult, ALU.mult).then_inc(x_full, 1)

                def x_tile_low(d):
                    dve.wait_ge(x_hi, (l * 4 + 2) * KD + d + 1)
                    V.tensor_tensor(xl[:, d, :], full[:, d % 2, :], xh[:, d, :].bitcast(F32),
                                    ALU.subtract).then_inc(x_rdy, 1)

                def low_unit(u):
                    low(base + u, u % 4, u % 2, KD // 2 if units_of(TILE["fc"])[0] in (u, u - 1) else KD)

                low_unit(2)
                dve.wait_ge(pre_r, l * 3 + 2)
                dve.wait_ge(m_load[0], l * (16 * N_MLOAD) + 16 * N_MLOAD)
                rotated = 0
                for u in range(2, N_AHEAD + 3):
                    if u > 2:
                        low_unit(u)
                    if u == 2:
                        ssm_input(0)
                    if u == 3:
                        ssm_input(1)
                        for i in range(2):
                            mlink(V.tensor_tensor(cosr[:, i, :], cosr[:, i, :], rstd[:, :], ALU.mult))
                    m = u - 3
                    name = COLS[m][0] if m >= TILE["fc"] else ""
                    if name == "fc":
                        forget(m)
                    elif name == "ka":
                        dve.wait_ge(kz_zero, l + 1)
                        rotate(m, rotated, 1.0, [(kz[64 * a:64 * a + 64, 2 * kv + a, :], slice(64 * kv, 64 * kv + 64))
                                                 for kv in range(2) for a in range(2)])
                        rotated += 1
                    elif name[:2] == "qa":
                        rotate(m, rotated, SCALE, [(qa[:, int(name[2]), :], slice(0, P))])
                        rotated += 1
                    elif name == "va":
                        value_columns(m, 0)
                    if m == TILE["fc"] + 2:
                        forget_sum()
                    if u in SCAN_AHEAD:
                        ssm_scan(SCAN_AHEAD[u])
                    if u in TURN_AHEAD:
                        ssm_turn(TURN_AHEAD[u])
                for s_ in range(N_ITEMS + LAG_N):
                    if s_ < N_ITEMS:
                        maxes(s_)
                    if s_ >= LAG_N:
                        norms(s_ - LAG_N)
                    if s_ in SCAN_AT:
                        ssm_scan(SCAN_AT[s_])
                    if s_ in TURN_AT:
                        ssm_turn(TURN_AT[s_])
                    if s_ - 2 in PROJECT_AT:
                        m = PROJECT_AT[s_ - 2]
                        if COLS[m][0][0] == "v":
                            value_columns(m, 1 + int(COLS[m][0][2]))
                        else:
                            fox_tile(m, [n_ for n_, _ in COLS if n_[:2] in ("kc", "qc")].index(COLS[m][0]))
                        if m + 2 < N_COLS:
                            low_unit(units_of(m + 2)[0])
                    if s_ == 6:
                        skip(0)
                    if s_ in GELU_AT:
                        T = GELU_AT.index(s_)
                        if T:
                            skip(1)
                        y, a2, z = us[:, T, :], sig[:, 0, :], sig[:, 1, :]
                        dve.wait_ge(y0_rdy, l * 2 + T + 1)
                        mlink(V.tensor_tensor(a2, y, y, ALU.mult))
                        mlink(V.tensor_scalar(a2, a2, 0.044715, 1.0, ALU.mult, ALU.add))
                        mlink(V.tensor_tensor(z, a2, y, ALU.mult))
                        V.tensor_scalar(z, z, -25.0, None, ALU.max).then_inc(gl_v, 1)
                    if s_ - 2 in GELU_AT:
                        T = GELU_AT.index(s_ - 2)
                        dve.wait_ge(gl_a, l * 12 + 3 * T + 3)
                        V.tensor_tensor(us[:, T, :], us[:, T, :], sig[:, 1, :], ALU.mult).then_inc(gl_v, 1)
                    if s_ == 20:
                        dve.wait_ge(gl_mm, l * 2 + 2)
                        for m in range(2):
                            V.tensor_scalar(gst[:, m, :], ps[GLU_BANK[m]][:, :],
                                            prm[:, bass.ds(R_GLUB + l * 2 + m, 1)], -40.0,
                                            ALU.add, ALU.max).then_inc(gl_lg, 1)
                    if s_ in (21, 22):
                        m = s_ - 21
                        dve.wait_ge(gl_a, l * 12 + 9 + 3 * m)
                        V.tensor_tensor(us[:, m, :], us[:, m, :], gst[:, m, :], ALU.mult).then_inc(gl_v, 1)
                    if s_ in XLO_AT:
                        x_tile_low(XLO_AT[s_])
                    if s_ in XHI_AT:
                        x_tile(XHI_AT[s_])
                    if s_ == 31:
                        low_first(l, U_OUT, 0)
                        low_first(l, U_OUT, 1)
                x_tile(6)
                x_tile(7)
                x_tile_low(6)
                x_tile_low(7)

                def out_four(j, i0):
                    for i in range(i0, 4):
                        low(l * U_LAYER + j * 4 + U_OUT + i, i, i % 2, KD)
                        d = j * 4 + i - 2
                        out_tile(l, l * (3 * KD) + KD + d, yM[:, bass.ds(d, 1), :].rearrange("p a n -> p (a n)"), d,
                                 1.0, OUT[i % 2], 3, i0 == 2 and i == 2)

                out_four(0, 2)
                with dve.Fori(1, N_OUT // 4) as j:
                    out_four(j, 0)
                for i in (2, 3):
                    out_tile(l, l * (3 * KD) + KD + 4 + i, yM[:, 4 + i, :], 4 + i, 1.0, OUT[i % 2], 3, False)
                assert mstep[0] == M_STEPS, (mstep[0], M_STEPS)

            M_STEPS = 8 + 2 + 5 + 2 * SWA_PAIRS + 4 + 4 * SWA_PAIRS * TOK + FOX_HEADS * TOK + 3
            with dve.Fori(0, DEPTH) as l:
                low_first(l, U_GU1, 0)
                for d in range(KD):
                    x_low(l, "ffn1", d)
                    if d == 1:
                        low_first(l, U_GU1, 1)
                ffn(l, U_GU1, U_DOWN1, 0, 0, 1)
                post_norm(l, 0, lambda d: yF[:, d, :], "mixer", U_IN)
                mixer(l)
                post_norm(l, 1, lambda d: yM[:, d, :], "ffn2", U_GU2)
                ffn(l, U_GU2, U_DOWN2, 1, 2 * KD, 5)
                post_norm(l, 2, lambda d: yF[:, d, :])

        @block.gpsimd
        def _(pool):
            G = nc.gpsimd

            def await_(semaphore, value):
                pool.wait_ge(semaphore, value)
                pool.sem_inc(pool_gate, 1)

            (LR, LI, LDT, DT, MAG, TH, KK, RR, SN, SH, CS, ABR, ABI, T1, T2, DEN, ZR, ZI) = range(18)
            pool.memset(fbias[:, :], 0.0).then_inc(pool_c, 1)
            pool.wait_ge(pool_c, 1)
            pool.dma_start(fbias[P - FOX_HEADS:P, :], fox_f_bias.rearrange("l h -> h l"),
                           allow_slow_non_contiguous=True).then_inc(s_small, 16)
            pool.dma_start(sinks[:, :, :].rearrange("p l h -> p (l h)"),
                           swa_sinks.rearrange("l h -> (l h)").unsqueeze(0).to_broadcast([P, DEPTH * SWA_HEADS]))\
                .then_inc(s_small, 16)
            pool.wait_ge(s_ssm, 4)
            LOG1, LOG32 = 5, 4
            batch_steps = 2 + 2 * (LOG1 + LOG32)
            with pool.Fori(0, DEPTH) as l:
                n = [0]
                layer0 = l * (batch_steps + ST * 4) + 1

                def settle(ins):
                    n[0] += 1
                    ins.then_inc(pool_c, 1)
                    await_(pool_c, layer0 + n[0])

                def wide(i, w):
                    return wk[:, i, :].unsqueeze(2).to_broadcast([P, ST, w])

                def doubling(t, log):
                    G.memset(t[:, 0, :, 0:1], 1.0)
                    settle(G.memset(t[:, 1, :, 0:1], 0.0))
                    for w in [2 ** i for i in range(log)]:
                        lo, hi = slice(0, w), slice(w, 2 * w)
                        a = tabt[:, 0, 0:ST * w].rearrange("p (c w) -> p c w", w=w)
                        b = tabt[:, 1, 0:ST * w].rearrange("p (c w) -> p c w", w=w)
                        G.tensor_tensor(a, t[:, 1, :, lo], wide(1, w), ALU.mult)
                        G.tensor_tensor(b, t[:, 1, :, lo], wide(0, w), ALU.mult)
                        G.tensor_tensor(t[:, 0, :, hi], t[:, 0, :, lo], wide(0, w), ALU.mult)
                        G.tensor_tensor(t[:, 1, :, hi], t[:, 0, :, lo], wide(1, w), ALU.mult)
                        G.tensor_tensor(wk[:, 2:4, :], wk[:, 0:2, :], wk[:, 0:2, :], ALU.mult)
                        settle(G.tensor_tensor(wk[:, 4, :], wk[:, 0, :], wk[:, 1, :], ALU.mult))
                        G.tensor_tensor(t[:, 0, :, hi], t[:, 0, :, hi], a, ALU.subtract)
                        G.tensor_tensor(t[:, 1, :, hi], t[:, 1, :, hi], b, ALU.add)
                        G.tensor_tensor(wk[:, 0, :], wk[:, 2, :], wk[:, 3, :], ALU.subtract)
                        settle(G.tensor_tensor(wk[:, 1, :], wk[:, 4, :], wk[:, 4, :], ALU.add))

                G.tensor_copy(wk[:, 0, :], ssm[:, CS, bass.ds(l * ST, ST)])
                G.tensor_copy(wk[:, 1, :], ssm[:, SN, bass.ds(l * ST, ST)])
                doubling(tab1, LOG1)
                doubling(tab32, LOG32)
                assert n[0] == batch_steps
                with pool.Fori(0, ST) as c:
                    for half in range(2):
                        def fine(r):
                            return tab1[:, r, bass.ds(c, 1), :].to_broadcast([P, 8, 32])

                        def coarse(r):
                            return tab32[:, r, bass.ds(c, 1), 8 * half:8 * half + 8]\
                                .rearrange("p c a -> p (c a)").unsqueeze(2).to_broadcast([P, 8, 32])

                        def grid(t, r):
                            return t[:, r, :].rearrange("p (a b) -> p a b", b=32)

                        G.tensor_tensor(grid(tabw, 0), coarse(0), fine(0), ALU.mult)
                        G.tensor_tensor(grid(tabt, 0), coarse(1), fine(1), ALU.mult)
                        G.tensor_tensor(grid(tabw, 1), coarse(0), fine(1), ALU.mult)
                        G.tensor_tensor(grid(tabt, 1), coarse(1), fine(0), ALU.mult).then_inc(pool_c, 1)
                        k = layer0 + batch_steps + c * 4 + 2 * half
                        await_(pool_c, k + 1)
                        G.tensor_tensor(tabw[:, 0, :], tabw[:, 0, :], tabt[:, 0, :], ALU.subtract)
                        G.tensor_tensor(tabw[:, 1, :], tabw[:, 1, :], tabt[:, 1, :], ALU.add).then_inc(pool_c, 1)
                        await_(pool_c, k + 2)
                        pool.dma_start(tables[bass.ds(l * ST + c, 1), :, :, half * (SEQ // 2):(half + 1) * (SEQ // 2)]
                                       .rearrange("c p r s -> p (c r) s"), tabw[:, :, :]).then_inc(tab_st, 16)
                        await_(tab_st, l * (32 * ST) + c * 32 + half * 16 + 16)
            pool.wait_ge(s_small, 32)
            setup = 1 + DEPTH * (batch_steps + ST * 4)

            def load_table(l, t):
                pool.dma_start(tab[:, t % 2, :, :],
                               tables[bass.ds(l * ST + t, 1)].rearrange("c p r s -> p (c r) s")).then_inc(tab_ld[t % 2], 16)

            with pool.Fori(0, DEPTH) as l:
                n = [0]

                def settle(ins):
                    n[0] += 1
                    ins.then_inc(pool_c, 1)
                    await_(pool_c, l * POOL_STEPS + setup + n[0])

                await_(y_used, l * (3 * KD) + KD + 2)
                for ri, (b, c) in enumerate(((b_re, c_re), (b_im, c_im))):
                    for g in range(2):
                        pool.dma_start(bnat[64 * g:64 * g + 64, ri, :, :],
                                       b[bass.ds(l, 1)].rearrange("a (t g) s c -> g s (a t) c", g=2)[g]).then_inc(m_load[1], 16)
                    pool.dma_start(cnat[:, ri, :, :],
                                   c[bass.ds(l, 1)].rearrange("a (T g) c s -> (g c) (a T) s", T=2)).then_inc(m_load[1], 16)
                pool.dma_start(cmask[:, :], const[:, K_CMASK:K_COS]).then_inc(m_load[0], 16)
                pool.dma_start(view2(cosr[:, :, :]), const[:, K_COS:K_ALL]).then_inc(m_load[0], 16)
                pool.dma_start(gluw[:, :, :], glu_w[bass.ds(l, 1)].rearrange("a (k p) n -> p (a k) n", p=P)).then_inc(m_load[0], 16)
                load_table(l, 0)
                load_table(l, 1)
                await_(m_load[1], l * 96 + 96)
                zr = ssm[:, ZR, bass.ds(l * ST, ST)].unsqueeze(2).to_broadcast([P, ST, 16])
                zi = ssm[:, ZI, bass.ds(l * ST, ST)].unsqueeze(2).to_broadcast([P, ST, 16])
                t1 = gst[:, 0, 0:P].rearrange("p (a b) -> p a b", b=16)
                t2 = gst[:, 0, P:2 * P].rearrange("p (a b) -> p a b", b=16)
                G.memset(bbd[:, :, :, :], 0.0)
                for ri in range(2):
                    G.tensor_tensor(t1, bnat[:, ri, :, :], zr, ALU.mult)
                    settle(G.tensor_tensor(t2, bnat[:, 1 - ri, :, :], zi, ALU.mult))
                    for g in range(2):
                        r = slice(64 * g, 64 * g + 64)
                        settle(G.tensor_tensor(bbd[r, ri, :, 16 * g:16 * g + 16], t1[r], t2[r],
                                               ALU.add if ri else ALU.subtract))
                pool.sem_inc(bb_rdy, 1)
                await_(m_load[0], l * 48 + 48)
                for ri in range(2):
                    for T in range(2):
                        for g in range(2):
                            last = G.tensor_tensor(cbd[:, ri * 2 + T, g * 64:g * 64 + 64], cnat[:, ri, T, :],
                                                   cmask[:, g * 64:g * 64 + 64], ALU.mult)
                settle(last)
                pool.sem_inc(bb_rdy, 1)
                G.memset(kz[:, :, :], 0.0).then_inc(kz_zero, 1)
                await_(kz_zero, l + 1)
                G.memset(kf[HD:HD + 2, :, :], 1.0)
                settle(G.memset(qf[HD:HD + 2, :, :], 1.0))
                for t in range(ST):
                    g = l * ST + t
                    await_(sc_rdy, (g + 1) * 2)
                    if t:
                        await_(sy_mm, g)
                    C, S = tab[:, t % 2, 0, :], tab[:, t % 2, 1, :]
                    im_s, im_c = view2(tabw[:, :, :]), view2(tabt[:, :, :])
                    G.tensor_tensor(hst[:, 0, :], gst[:, 0, :], C, ALU.mult)
                    G.tensor_tensor(im_s, gst[:, 1, :], S, ALU.mult)
                    G.tensor_tensor(hst[:, 1, :], gst[:, 0, :], S, ALU.mult)
                    settle(G.tensor_tensor(im_c, gst[:, 1, :], C, ALU.mult))
                    G.tensor_tensor(hst[:, 0, :], hst[:, 0, :], im_s, ALU.subtract)
                    G.tensor_tensor(hst[:, 1, :], hst[:, 1, :], im_c, ALU.add).then_inc(hs_rdy, 1)
                    if t + 2 < ST:
                        await_(hs_rdy, g + 1)
                        load_table(l, t + 2)
                    if 1 <= t <= FOX_HEADS:
                        await_(cum_rdy, l + 1)
                        h = t - 1
                        r = P - FOX_HEADS + h
                        pool.dma_start(qf[HD:HD + 1, h, :], full[r:r + 1, 0, :]).then_inc(aug_ld, 16)
                        pool.dma_start(kf[HD + 1:HD + 2, h, :], full[r:r + 1, 1, :]).then_inc(aug_ld, 16)
                assert n[0] == POOL_STEPS


EXP_LN_SET = 6
POOL_STEPS = 2 + 4 + 2 + ST
SQUARE_AT = {12: 0, 13: 1, 16: 2, 20: 3, 22: 4, 23: 5, 28: 6}
SUM_AT = {13: 0, 14: 1, 17: 2, 21: 3, 23: 4, 24: 5, 29: 6}
GELU_AT = (8, 17)
PROJECT_AT = {0: 9, 4: 10, 8: 11, 12: 12, 16: 13, 19: 14}
VALUES_AT = (None, 8, 20)
SSM_IN_AHEAD, SSM_IN_AT = {2: 0, 4: 1, 7: 2}, {0: 3, 3: 4, 6: 5, 8: 6, 11: 7}
SSM_OUT_AHEAD, SSM_OUT_AT = {6: 0, 8: 1}, {2: 2, 5: 3, 8: 4, 10: 5, 13: 6, 16: 7}
TURN_AHEAD, TURN_AT = {4: 0, 6: 1, 9: 2}, {0: 3, 3: 4, 6: 5, 8: 6, 11: 7}
SCAN_AHEAD, SCAN_AT = {5: 0, 7: 1, 10: 2}, {1: 3, 4: 4, 7: 5, 9: 6, 12: 7}
XHI_AT = {23: 0, 24: 1, 25: 2, 26: 3, 28: 4, 29: 5}
XLO_AT = {24: 0, 25: 1, 26: 2, 27: 3, 29: 4, 30: 5}


_INS = ["x", "norm_gains", "ffn1_gate", "ffn1_up", "ffn1_down", "w_in", "swa_sinks", "ssm_lambda_re",
        "ssm_lambda_im", "ssm_log_dt", "ssm_b_re", "ssm_b_im", "ssm_c_re", "ssm_c_im", "ssm_d", "ssm_glu_w",
        "ssm_glu_b", "fox_f_bias", "mix_norm_gain", "w_out", "ffn2_gate", "ffn2_up", "ffn2_down"]


def kernel(**inputs):
    import concourse.bacc as bacc
    from concourse.bass_utils import run_bass_kernel_spmd

    nc = bacc.Bacc("TRN2", target_bir_lowering=False, num_devices=1)
    arrays, args = {}, []
    for name in _INS:
        a = np.ascontiguousarray(inputs[name])
        arrays[f"in_{name}"] = a
        args.append(nc.dram_tensor(f"in_{name}", a.shape, mybir.dt.from_np(a.dtype), kind="ExternalInput").ap())
    arrays["const"] = constants()
    args.append(nc.dram_tensor("const", (P, K_ALL), F32, kind="ExternalInput").ap())
    args.append(nc.dram_tensor("out", (1, SEQ, D_MODEL), F32, kind="ExternalOutput").ap())
    build(nc, *args)
    r = run_bass_kernel_spmd(nc, [arrays], core_ids=[0])
    return r.results[0]["out"]
```
